# Optimizing a Trainium2 kernel written in Bass

```python
import math
import jax, jax.numpy as jnp
from jax import lax
import numpy as np

D_MODEL = 1024
BATCH = 1
SEQ = 256
DEPTH = 1

ATTN_HEADS = 8
ATTN_HEAD_DIM = 128
ATTN_WIDTH = ATTN_HEADS * ATTN_HEAD_DIM
MOBA_BLOCK = 256
MOBA_TOPK = 3
Q_CHUNK = 128
REL_BUCKETS = 32
REL_MAX_DIST = 128
SSM_EXPAND = 2
SSM_INNER = SSM_EXPAND * D_MODEL
SSM_HEAD_DIM = 64
SSM_HEADS = SSM_INNER // SSM_HEAD_DIM
SSM_GROUPS = 8
SSM_HEADS_PER_GROUP = SSM_HEADS // SSM_GROUPS
SSM_STATE = 128
SSM_CONV = 4
SSM_CHUNK = 256
SSM_CONV_DIM = SSM_INNER + 2 * SSM_GROUPS * SSM_STATE
FFN_HIDDEN = 2816
FFN_RES = 0.5
N_BRANCH = 2
IN_PROJ_DIM = 3 * ATTN_WIDTH + SSM_INNER + SSM_CONV_DIM + SSM_HEADS + N_BRANCH * D_MODEL
N_MOD = 9
RMS_EPS = 1e-6

kernel_name = 'hybrid_moba_ssd_macaron_block'

def rms_norm(x, g):
    xf = x.astype(jnp.float32)
    y = xf * lax.rsqrt(jnp.mean(xf * xf, axis=-1, keepdims=True) + RMS_EPS)
    return (y * g.astype(jnp.float32)).astype(x.dtype)

def modulate(h, shift, scale):
    return h * (1 + scale[:, None, :]) + shift[:, None, :]

def swiglu(h, w_in, w_out):
    a, b = jnp.split(h @ w_in, 2, axis=-1)
    return (jax.nn.silu(a) * b) @ w_out

def t5_bucket(rel):
    n = jnp.maximum(rel, 0)
    max_exact = REL_BUCKETS // 2
    nf = jnp.maximum(n, 1).astype(jnp.float32)
    large = max_exact + (jnp.log(nf / max_exact) / math.log(REL_MAX_DIST / max_exact)
                         * (REL_BUCKETS - max_exact)).astype(jnp.int32)
    large = jnp.minimum(large, REL_BUCKETS - 1)
    return jnp.where(n < max_exact, n, large)

def moba_attention(q, k, v, rel_bias):
    Bsz, S, H, Dh = q.shape
    nb = -(-S // MOBA_BLOCK)
    pad = nb * MOBA_BLOCK - S
    k = jnp.pad(k, ((0, 0), (0, pad), (0, 0), (0, 0)))
    v = jnp.pad(v, ((0, 0), (0, pad), (0, 0), (0, 0)))
    kb = k.transpose(0, 2, 1, 3).reshape(Bsz, H, nb, MOBA_BLOCK, Dh)
    vb = v.transpose(0, 2, 1, 3).reshape(Bsz, H, nb, MOBA_BLOCK, Dh)
    q = q.transpose(0, 2, 1, 3) * (Dh ** -0.5)
    kmean = jnp.mean(kb.astype(jnp.float32), axis=3)
    score = jnp.einsum('bhsd,bhnd->bhsn', q.astype(jnp.float32), kmean)
    cur = jnp.arange(S) // MOBA_BLOCK
    past = jnp.arange(nb)[None, :] < cur[:, None]
    score = jnp.where(past, score, -jnp.inf)
    topk = min(MOBA_TOPK, nb)
    _, idx = lax.top_k(score, topk)

    tab = rel_bias.T.astype(jnp.float32)
    nqc = S // Q_CHUNK
    q_c = q.reshape(Bsz, H, nqc, Q_CHUNK, Dh).transpose(2, 0, 1, 3, 4)
    idx_c = idx.reshape(Bsz, H, nqc, Q_CHUNK, topk).transpose(2, 0, 1, 3, 4)
    starts = jnp.arange(nqc, dtype=jnp.int32) * Q_CHUNK
    b_ix = jnp.arange(Bsz)[:, None, None, None]
    h_ix = jnp.arange(H)[None, :, None, None]
    offs = jnp.arange(MOBA_BLOCK, dtype=jnp.int32)
    nsel = topk * MOBA_BLOCK

    def one_chunk(args):
        qq, ii, start = args
        blk = start // MOBA_BLOCK
        q_pos = start + jnp.arange(Q_CHUNK, dtype=jnp.int32)
        kg = kb[b_ix, h_ix, ii]
        vg = vb[b_ix, h_ix, ii]
        lg = jnp.einsum('bhqd,bhqjkd->bhqjk', qq, kg).astype(jnp.float32)
        kpos_g = ii[..., None] * MOBA_BLOCK + offs
        rel_g = q_pos[None, None, :, None, None] - kpos_g
        lg = lg + tab[h_ix[..., None], t5_bucket(rel_g)]
        lg = jnp.where((ii < blk)[..., None], lg, -jnp.inf)
        ko = lax.dynamic_index_in_dim(kb, blk, axis=2, keepdims=False)
        vo = lax.dynamic_index_in_dim(vb, blk, axis=2, keepdims=False)
        lo = jnp.einsum('bhqd,bhkd->bhqk', qq, ko).astype(jnp.float32)
        rel_o = q_pos[:, None] - (blk * MOBA_BLOCK + offs)[None, :]
        lo = lo + tab[:, t5_bucket(rel_o)][None]
        lo = jnp.where(rel_o >= 0, lo, -jnp.inf)
        logits = jnp.concatenate([lg.reshape(Bsz, H, Q_CHUNK, nsel), lo], axis=-1)
        p = jax.nn.softmax(logits, axis=-1).astype(vb.dtype)
        pg = p[..., :nsel].reshape(Bsz, H, Q_CHUNK, topk, MOBA_BLOCK)
        po = p[..., nsel:]
        return (jnp.einsum('bhqjk,bhqjkd->bhqd', pg, vg)
                + jnp.einsum('bhqk,bhkd->bhqd', po, vo))

    out = lax.map(one_chunk, (q_c, idx_c, starts))
    return out.transpose(1, 0, 3, 2, 4).reshape(Bsz, S, H * Dh)

def mamba2_ssd(z, xbc, dt_raw, conv_w, conv_b, dt_bias, a_log, d_skip, norm_w):
    Bsz, S, _ = xbc.shape
    G, HG, P, N, L = SSM_GROUPS, SSM_HEADS_PER_GROUP, SSM_HEAD_DIM, SSM_STATE, SSM_CHUNK
    xbc = lax.conv_general_dilated(xbc, conv_w[:, None, :], window_strides=(1,),
                                   padding=[(SSM_CONV - 1, 0)],
                                   dimension_numbers=('NWC', 'WIO', 'NWC'),
                                   feature_group_count=SSM_CONV_DIM) + conv_b
    xbc = jax.nn.silu(xbc)
    xs, bm, cm = jnp.split(xbc, [SSM_INNER, SSM_INNER + G * N], axis=-1)
    dt = jax.nn.softplus(dt_raw.astype(jnp.float32) + dt_bias.astype(jnp.float32))
    a = -jnp.exp(a_log.astype(jnp.float32)).reshape(G, HG)
    nc = -(-S // L)
    pad = nc * L - S

    def to_chunks(t):
        t = jnp.pad(t, [(0, 0), (0, pad)] + [(0, 0)] * (t.ndim - 2))
        return t.reshape((Bsz, nc, L) + t.shape[2:]).swapaxes(0, 1)

    xf = xs.astype(jnp.float32)
    xc = to_chunks(xf.reshape(Bsz, S, G, HG, P))
    bc = to_chunks(bm.astype(jnp.float32).reshape(Bsz, S, G, N))
    cc = to_chunks(cm.astype(jnp.float32).reshape(Bsz, S, G, N))
    dtc = to_chunks(dt.reshape(Bsz, S, G, HG))
    tril = jnp.tril(jnp.ones((L, L), dtype=bool))

    def step(state, inp):
        x_, b_, c_, dt_ = inp
        cum = jnp.cumsum(dt_ * a, axis=1)
        seg = cum[:, :, None] - cum[:, None, :]
        decay = jnp.exp(jnp.where(tril[None, :, :, None, None], seg, -jnp.inf))
        cb = jnp.einsum('btgn,bsgn->btsg', c_, b_)
        w = cb[..., None] * decay * dt_[:, None]
        y = jnp.einsum('btsgh,bsghp->btghp', w, x_)
        y = y + jnp.einsum('btgn,bghpn->btghp', c_, state) * jnp.exp(cum)[..., None]
        to_end = jnp.exp(cum[:, -1:] - cum) * dt_
        state = (jnp.exp(cum[:, -1])[..., None, None] * state
                 + jnp.einsum('bsgn,bsgh,bsghp->bghpn', b_, to_end, x_))
        return state, y

    state0 = jnp.zeros((Bsz, G, HG, P, N), jnp.float32)
    _, ys = lax.scan(step, state0, (xc, bc, cc, dtc))
    y = ys.swapaxes(0, 1).reshape(Bsz, nc * L, SSM_INNER)[:, :S]
    y = y + (xf.reshape(Bsz, S, SSM_HEADS, P)
             * d_skip.astype(jnp.float32)[:, None]).reshape(Bsz, S, SSM_INNER)
    g = (y * jax.nn.silu(z.astype(jnp.float32))).reshape(Bsz, S, G, SSM_INNER // G)
    g = g * lax.rsqrt(jnp.mean(g * g, axis=-1, keepdims=True) + RMS_EPS)
    return (g.reshape(Bsz, S, SSM_INNER) * norm_w.astype(jnp.float32)).astype(z.dtype)

def hybrid_mixer(u, w_in, rel_bias, conv_w, conv_b, dt_bias, a_log, d_skip, ssm_norm_w,
                 proj_a, proj_b, w_out):
    Bsz, S, _ = u.shape
    sizes = (ATTN_WIDTH, ATTN_WIDTH, ATTN_WIDTH, SSM_INNER, SSM_CONV_DIM, SSM_HEADS, D_MODEL, D_MODEL)
    cuts = np.cumsum(sizes)[:-1].tolist()
    q, k, v, z, xbc, dt_raw, gate_a, gate_b = jnp.split(u @ w_in, cuts, axis=-1)
    heads = lambda t: t.reshape(Bsz, S, ATTN_HEADS, ATTN_HEAD_DIM)
    y_a = moba_attention(heads(q), heads(k), heads(v), rel_bias) @ proj_a
    y_b = mamba2_ssd(z, xbc, dt_raw, conv_w, conv_b, dt_bias, a_log, d_skip,
                     ssm_norm_w) @ proj_b
    s_a = jax.nn.sigmoid(gate_a.astype(jnp.float32)).astype(u.dtype)
    s_b = jax.nn.sigmoid(gate_b.astype(jnp.float32)).astype(u.dtype)
    return (s_a * y_a + s_b * y_b) @ w_out

def setup_inputs(seed: int = 0) -> dict:
    key = jax.random.key(seed)
    ks = jax.random.split(key, 26)
    f32 = jnp.float32
    Ld = DEPTH
    nrm = lambda k, shape, s: jax.random.normal(k, shape, f32) * s
    gain = lambda k, shape: 1.0 + 0.05 * jax.random.normal(k, shape, f32)
    dt0 = jnp.exp(jax.random.uniform(ks[13], (Ld, SSM_HEADS), f32, math.log(1e-3), math.log(1e-1)))
    return {
        'x': nrm(ks[0], (BATCH, SEQ, D_MODEL), 1.0),
        'c': nrm(ks[1], (BATCH, D_MODEL), 1.0),
        'w_ada': nrm(ks[2], (Ld, D_MODEL, N_MOD * D_MODEL), 0.5 * D_MODEL ** -0.5),
        'b_ada': nrm(ks[3], (Ld, N_MOD * D_MODEL), 0.02),
        'ffn1_norm_pre': gain(ks[4], (Ld, D_MODEL)),
        'ffn1_w_in': nrm(ks[5], (Ld, D_MODEL, 2 * FFN_HIDDEN), D_MODEL ** -0.5),
        'ffn1_w_out': nrm(ks[6], (Ld, FFN_HIDDEN, D_MODEL), FFN_HIDDEN ** -0.5),
        'ffn1_norm_post': gain(ks[7], (Ld, D_MODEL)),
        'mix_norm_pre': gain(ks[8], (Ld, D_MODEL)),
        'w_in_mix': nrm(ks[9], (Ld, D_MODEL, IN_PROJ_DIM), D_MODEL ** -0.5),
        'rel_bias': nrm(ks[10], (REL_BUCKETS, ATTN_HEADS), 0.5),
        'conv_w': nrm(ks[11], (Ld, SSM_CONV, SSM_CONV_DIM), SSM_CONV ** -0.5),
        'conv_b': nrm(ks[12], (Ld, SSM_CONV_DIM), 0.01),
        'dt_bias': dt0 + jnp.log(-jnp.expm1(-dt0)),
        'a_log': jnp.log(jax.random.uniform(ks[14], (Ld, SSM_HEADS), f32, 1.0, 16.0)),
        'd_skip': gain(ks[15], (Ld, SSM_HEADS)),
        'ssm_norm_w': gain(ks[16], (Ld, SSM_INNER)),
        'proj_a': nrm(ks[17], (Ld, ATTN_WIDTH, D_MODEL), ATTN_WIDTH ** -0.5),
        'proj_b': nrm(ks[18], (Ld, SSM_INNER, D_MODEL), SSM_INNER ** -0.5),
        'w_out_mix': nrm(ks[19], (Ld, D_MODEL, D_MODEL), D_MODEL ** -0.5),
        'mix_norm_post': gain(ks[20], (Ld, D_MODEL)),
        'ffn2_norm_pre': gain(ks[21], (Ld, D_MODEL)),
        'ffn2_w_in': nrm(ks[22], (Ld, D_MODEL, 2 * FFN_HIDDEN), D_MODEL ** -0.5),
        'ffn2_w_out': nrm(ks[23], (Ld, FFN_HIDDEN, D_MODEL), FFN_HIDDEN ** -0.5),
        'ffn2_norm_post': gain(ks[24], (Ld, D_MODEL)),
    }

def reference(x, c, w_ada, b_ada, ffn1_norm_pre, ffn1_w_in, ffn1_w_out, ffn1_norm_post,
              mix_norm_pre, w_in_mix, rel_bias, conv_w, conv_b, dt_bias, a_log, d_skip,
              ssm_norm_w, proj_a, proj_b, w_out_mix, mix_norm_post,
              ffn2_norm_pre, ffn2_w_in, ffn2_w_out, ffn2_norm_post):
    h = x
    cs = jax.nn.silu(c)
    for l in range(DEPTH):
        mod = cs @ w_ada[l] + b_ada[l]
        sh1, sc1, g1, shm, scm, gm, sh2, sc2, g2 = jnp.split(mod, N_MOD, axis=-1)
        u = modulate(rms_norm(h, ffn1_norm_pre[l]), sh1, sc1)
        h = h + FFN_RES * g1[:, None] * rms_norm(swiglu(u, ffn1_w_in[l], ffn1_w_out[l]), ffn1_norm_post[l])
        u = modulate(rms_norm(h, mix_norm_pre[l]), shm, scm)
        y = hybrid_mixer(u, w_in_mix[l], rel_bias, conv_w[l], conv_b[l], dt_bias[l], a_log[l],
                         d_skip[l], ssm_norm_w[l], proj_a[l], proj_b[l], w_out_mix[l])
        h = h + gm[:, None] * rms_norm(y, mix_norm_post[l])
        u = modulate(rms_norm(h, ffn2_norm_pre[l]), sh2, sc2)
        h = h + FFN_RES * g2[:, None] * rms_norm(swiglu(u, ffn2_w_in[l], ffn2_w_out[l]), ffn2_norm_post[l])
    return h


_drawn_inputs = setup_inputs


def setup_inputs(seed=0):
    import zlib

    import numpy as np

    out = dict(_drawn_inputs(seed))
    spreads = {}
    factors = {'ffn1_norm_pre': 5.079,
     'ffn1_norm_post': 7.493,
     'conv_b': 8.0,
     'd_skip': 8.0,
     'ssm_norm_w': 3.954,
     'mix_norm_post': 3.851,
     'ffn2_norm_pre': 5.58,
     'ffn2_norm_post': 8.0,
     'rel_bias': 3.508}
    for name, (base, spread) in spreads.items():
        noise = np.random.default_rng([zlib.crc32(name.encode()), seed]).standard_normal(out[name].shape)
        drawn = base * np.exp(spread * noise) if base else spread * noise
        out[name] = __import__('jax').numpy.asarray(drawn.astype(out[name].dtype))
    for name, factor in factors.items():
        out[name] = (out[name] * factor).astype(out[name].dtype)
    return out
```

```python
from contextlib import ExitStack

import numpy as np

import concourse.bass as bass
from concourse import mybir

ALU = mybir.AluOpType
ACT = mybir.ActivationFunctionType
F32 = mybir.dt.float32
F32R = mybir.dt.float32r
AX_X = mybir.AxisListType.X

P = 128
T = 256
D = 1024
KT = D // P
H = 8
HID = 2816
INNER = 2048
SH = 32
G = 8
HG = SH // G
HP = INNER // SH
TAPS = 4
BUCKETS = 32
EPS = 1e-6
NEG = -1e30
MODS = 9
COL_Q, COL_K, COL_V = 0, D, 2 * D
COL_Z = 3 * D
COL_X = COL_Z + INNER
COL_B = COL_X + INNER
COL_C = COL_B + G * P
COL_DT = COL_C + G * P
COL_GA = COL_DT + SH
COL_GB = COL_GA + D
SH1, SC1, G1, SHM, SCM, GM, SH2, SC2, G2 = range(MODS)

PAIRS = HID // (2 * P)
RAW = 3
GR = 2 * RAW
U_F1IN = 0
U_F1OUT = U_F1IN + 2 * PAIRS
U_QKV = U_F1OUT + PAIRS
U_SSD = U_QKV + 12
U_GA = U_SSD + 3 * G
U_PA = U_GA + 4
U_PB = U_PA + 4
U_GB = U_PB + 8
U_WO = U_GB + 4
U_F2IN = U_WO + 4
U_F2OUT = U_F2IN + 2 * PAIRS
UNITS = U_F2OUT + PAIRS


def build(nc, x, c, w_ada, b_ada, norms, ffn_in, ffn_out, w_in_mix, rel_bias, conv_w, conv_b,
          dt_bias, a_log, d_skip, ssm_norm_w, proj_a, proj_b, w_out_mix,
          k_ident, k_flip, k_mask, k_onehot, k_causal, bias_rows, out):
    with ExitStack() as ctx:
        def sb(name, shape, dt=F32):
            return ctx.enter_context(nc.sbuf_tensor(name, shape, dt))

        def sem(name):
            return ctx.enter_context(nc.semaphore(name))

        ps = ctx.enter_context(nc.psum_tensor("ps", [P, 8, 512], F32))

        raw = sb("raw", [P, RAW, 2048])
        w_high = sb("w_high", [P, GR, 1024], F32R)
        w_low = sb("w_low", [P, GR, 1024], F32R)
        u_high = sb("u_high", [P, KT, T], F32R)
        u_low = sb("u_low", [P, KT, T], F32R)
        in_high = sb("in_high", [P, 24, T], F32R)
        in_low = sb("in_low", [P, 24, T], F32R)
        hT = sb("hT", [P, KT, T])
        work = sb("work", [P, KT, T])
        ada_ring = sb("ada_ring", [P, 2, 2048])
        ada_acc = sb("ada_acc", [P, D])
        ada_acc1 = raw[:, 2, 0:D]
        scratch = sb("scratch", [P, 5632])
        ident = sb("ident", [P, P])
        flip = sb("flip", [P, P])
        mask = sb("mask", [P, 384])
        ones = sb("ones", [P, P])
        ones_d = sb("ones_d", [P, P])
        ones_g = sb("ones_g", [P, P])
        par1 = sb("par1", [P, P])
        par2 = sb("par2", [P, TAPS, 32])
        par3 = sb("par3", [P, 48])
        cs = sb("cs", [P, KT])
        mod = sb("mod", [P, MODS, KT])
        scale_in = sb("scale_in", [P, 3, KT])
        scale_out = sb("scale_out", [P, 3, KT])
        rms = sb("rms", [P, T])
        dtw = sb("dtw", [P, KT, SH])
        dtw_parts = sb("dtw_parts", [P, 2, KT, SH], F32R)
        dtw_high, dtw_low = dtw_parts[:, 0], dtw_parts[:, 1]
        dtb = sb("dtb", [P, SH])
        aexp = sb("aexp", [P, SH])
        dskip = sb("dskip", [P, INNER // P])
        dts = sb("dts", [P, 4, 2, SH])
        dt = sb("dt", [P, 2, SH])
        cum = sb("cum", [P, 2, SH])
        cum_high = sb("cum_high", [SH, T], F32R)
        cum_low = sb("cum_low", [SH, T], F32R)
        sel = dtw_parts[0:SH].rearrange("p a k h -> p (a k h)").rearrange("p (j n) -> p j n", j=HG)
        nmax = sb("nmax", [P, 4])
        rsum = sb("rsum", [P, 4])
        eps = sb("eps", [P, 1])
        rel_tab = sb("rel_tab", [BUCKETS, H])

        par = scratch[:, 4096:4480].rearrange("p (r n) -> p r n", r=3)
        onehot = scratch[0:BUCKETS, 4480:4864]
        causal = scratch[0:H, 4864:5248]
        silu_a = scratch[:, 4096:5632].rearrange("p (r n) -> p r n", r=3)
        toep = scratch[:, 0:2048].rearrange("p (h k) -> p h k", h=H)
        hankel = scratch[:, 2048:4096].rearrange("p (h k) -> p h k", h=H)
        qT = scratch[:, 2048:2560].rearrange("p (h q) -> p h q", h=2)
        kTt = scratch[:, 2560:3072].rearrange("p (h q) -> p h q", h=2)
        vT = scratch[:, 3072:3584].rearrange("p (h q) -> p h q", h=2)
        v_tok = scratch[:, 3584:4096].rearrange("p (h s d) -> p h s d", h=2, s=2)
        probs = scratch[:, 4096:4864].rearrange("p (h k) -> p h k", h=2)
        probsT = scratch[:, 4864:5632].rearrange("p (h k) -> p h k", h=2)
        conv = scratch[:, 0:1024].rearrange("p (c t) -> p c t", c=4)
        ssm_z = scratch[:, 1024:1536]
        yg = scratch[:, 1536:2048].rearrange("p (c t) -> p c t", c=2)
        decay = scratch[:, 2048:3584].rearrange("p (h t) -> p h t", h=HG)
        cbm = scratch[:, 3584:3968]
        xdt = scratch[:, 4096:4608].rearrange("p (s h d) -> p s h d", s=2, h=HG)
        gsq = scratch[:, 4608:5120].rearrange("p (c t) -> p c t", c=2)
        rms_g = scratch[:, 5120:5376]
        out_tok = scratch[:, 0:2048].rearrange("p (b s d) -> p b s d", b=4, s=2)
        gate_b = scratch[:, 0:1024].rearrange("p (r n) -> p r n", r=2)

        raw_loaded = [sem(f"raw_loaded{i}") for i in range(RAW)]
        high_ready, low_ready, used = sem("high_ready"), sem("low_ready"), sem("used")
        const_loaded, par_loaded, x_loaded = sem("const_loaded"), sem("par_loaded"), sem("x_loaded")
        c_loaded, c_turned, part_done = sem("c_loaded"), sem("c_turned"), sem("part_done")
        small_loaded, ones_set = sem("small_loaded"), sem("ones_set")
        onehot_loaded, bias_made, bias_copied, bias_stored, hankel_loaded, toep_turned, toep_ready = (
            sem("onehot_loaded"), sem("bias_made"), sem("bias_copied"), sem("bias_stored"),
            sem("hankel_loaded"), sem("toep_turned"), sem("toep_ready"))
        par_turned, par_copied, cs_ready = sem("par_turned"), sem("par_copied"), sem("cs_ready")
        x_turned, x_copied = sem("x_turned"), sem("x_copied")
        ada_loaded = [sem(f"ada_loaded{i}") for i in range(4)]
        ada_used, ada_ready, ada_summed, mod_ready = (
            sem("ada_used"), sem("ada_ready"), sem("ada_summed"), sem("mod_ready"))
        ada_step = sem("ada_step")
        squared, mean_done, root_ready, rms_ready = sem("squared"), sem("mean_done"), sem("root_ready"), sem("rms_ready")
        term_ready, h_ready = sem("term_ready"), sem("h_ready")
        scaled, u_hi, u_lo = sem("scaled"), sem("u_hi"), sem("u_lo")
        silu_done, s_done, s_hi, s_lo = sem("silu_done"), sem("s_done"), sem("s_hi"), sem("s_lo")
        dtw_hi, dtw_lo, dt_done, dt_in, dt_act, dt_ready = (
            sem("dtw_hi"), sem("dtw_lo"), sem("dt_done"), sem("dt_in"), sem("dt_act"), sem("dt_ready"))
        cum_done, cum_copied, cum_turned, cum_hi, cum_lo = (
            sem("cum_done"), sem("cum_copied"), sem("cum_turned"), sem("cum_hi"), sem("cum_lo"))
        q_copied, k_copied, v_copied = sem("q_copied"), sem("k_copied"), sem("v_copied")
        scores_done, softmax_step, max_ready, exp_done, probs_ready = (
            sem("scores_done"), sem("softmax_step"), sem("max_ready"), sem("exp_done"), sem("probs_ready"))
        probs_turned, probsT_ready, v_ready, pv_done, o_hi, o_lo = (
            sem("probs_turned"), sem("probsT_ready"), sem("v_ready"), sem("pv_done"), sem("o_hi"), sem("o_lo"))
        sel_ready, own, skip_ready = sem("sel_ready"), sem("own"), sem("skip_ready")
        tap_done, taps_step, conv_done, conv_silu, z_silu = (
            sem("tap_done"), sem("taps_step"), sem("conv_done"), sem("conv_silu"), sem("z_silu"))
        ssd_in, ssd_cum, xdt_ready, cbm_ready, seg_done, decay_ready, w_ready = (
            sem("ssd_in"), sem("ssd_cum"), sem("xdt_ready"), sem("cbm_ready"), sem("seg_done"), sem("decay_ready"),
            sem("w_ready"))
        y_done, y_skip, y_gated, g_squared, g_mean, g_root, g_rms, g_normed, g_hi, g_lo = (
            sem("y_done"), sem("y_skip"), sem("y_gated"), sem("g_squared"), sem("g_mean"), sem("g_root"), sem("g_rms"),
            sem("g_normed"), sem("g_hi"), sem("g_lo"))
        gate_a_done, mixed_a, gate_b_done, gate_b_used, mixed_b, m_hi, m_lo = (
            sem("gate_a_done"), sem("mixed_a"), sem("gate_b_done"), sem("gate_b_used"), sem("mixed_b"), sem("m_hi"),
            sem("m_lo"))
        out_turned, out_copied, stored = sem("out_turned"), sem("out_copied"), sem("stored")

        GA_BANK = (0, 1, 2, 0)
        block = ctx.enter_context(nc.Block())

        def granule(n, g):
            return (2 * n + g) % GR

        def split_count(n, g, i, step):
            return 2 * n + g + 1 + 2 * step * i

        @block.sync
        def _(sp):
            def load(n, parts, i=0, step=0):
                if n >= RAW:
                    sp.wait_ge(low_ready, 2 * (n - RAW) + 2 + 2 * step * i)
                for dst, src in parts:
                    sp.dma_start(dst, src).then_inc(raw_loaded[n % RAW], 16)

            def halves(n):
                return [raw[:, n % RAW, g * 1024:(g + 1) * 1024] for g in range(2)]

            def col_unit(n, w, at, i=0, step=0):
                load(n, [(dst.rearrange("p (k n) -> p k n", k=4),
                          w[512 * g:512 * g + 512, bass.ds(at, 256)].rearrange("(k p) n -> p k n", p=P))
                         for g, dst in enumerate(halves(n))], i, step)

            def row_unit(n, w, at, i=0, step=0):
                load(n, [(dst, w[bass.ds(at + P * g, P), :]) for g, dst in enumerate(halves(n))], i, step)

            with nc.allow_non_contiguous_dma(reason="small"):
                sp.dma_start(ident[:], k_ident).then_inc(const_loaded, 16)
                sp.dma_start(par[0:8, 0, :], c.rearrange("a (r n) -> (a r) n", n=P)).then_inc(c_loaded, 16)
                sp.dma_start(work[:].rearrange("p k t -> p (k t)").rearrange("p (s d) -> p s d", s=2),
                             x[0].rearrange("(s p) d -> p s d", p=P)).then_inc(x_loaded, 16)
                sp.dma_start(par[8:80, 0, :], b_ada.rearrange("a (r n) -> (a r) n", n=P)).then_inc(par_loaded, 16)
                for m, g in enumerate(norms):
                    sp.dma_start(par[80 + 8 * m:88 + 8 * m, 0, :],
                                 g.rearrange("a (r n) -> (a r) n", n=P)).then_inc(par_loaded, 16)
            sp.wait_ge(ada_loaded[0], 32)

            def small_loads():
                with nc.allow_non_contiguous_dma(reason="small"):
                    for dst, src in (
                            (par[:, 1, :], conv_w[0].rearrange("t (r n) -> (t r) n", n=P)),
                            (par[0:32, 2, :], conv_b.rearrange("a (r n) -> (a r) n", n=P)),
                            (par[32:48, 2, :], ssm_norm_w.rearrange("a (r n) -> (a r) n", n=P)),
                            (flip[:], k_flip),
                            (mask[:], k_mask),
                            (dtw[:], w_in_mix[0][:, COL_DT:COL_DT + SH].rearrange("(k p) n -> p k n", p=P)),
                            (dtb[:], dt_bias.partition_broadcast(P)),
                            (aexp[:], a_log.partition_broadcast(P)),
                            (dskip[0:HP, :], d_skip[0].rearrange("(r s) -> s r", s=2)[0:1, :].partition_broadcast(HP)),
                            (dskip[HP:P, :], d_skip[0].rearrange("(r s) -> s r", s=2)[1:2, :].partition_broadcast(HP))):
                        sp.dma_start(dst, src).then_inc(small_loaded, 16)

            def ffn(f, u_in, u_out):
                w_in, w_out = ffn_in[f], ffn_out[f]

                def pair(p, i=0):
                    col_unit(u_in + 2 * p, w_in, 256 * p + 768 * i, i, 6)
                    if f == 0 and p == 0:
                        small_loads()
                    col_unit(u_in + 2 * p + 1, w_in, HID + 256 * p + 768 * i, i, 6)

                pair(0)
                if f == 0:
                    sp.wait_ge(ada_summed, 2)
                pair(1)
                with sp.Fori(0, (PAIRS - 2) // 3) as i:
                    for p in range(2, 5):
                        pair(p, i)
                with sp.Fori(0, PAIRS // 3) as i:
                    for u in range(3):
                        row_unit(u_out + u, w_out, 256 * u + 768 * i, i, 3)
                for u in range(PAIRS // 3 * 3, PAIRS):
                    row_unit(u_out + u, w_out, 256 * u)

            ffn(0, U_F1IN, U_F1OUT)
            with sp.Fori(0, H // 2) as i:
                for j, col in enumerate((COL_Q, COL_K, COL_V)):
                    col_unit(U_QKV + j, w_in_mix[0], col + 256 * i, i, 3)
            with sp.Fori(0, G) as g:
                col_unit(U_SSD, w_in_mix[0], COL_X + 256 * g, g, 3)
                both = raw[:, (U_SSD + 1) % RAW, :].rearrange("p (k n) -> p k n", k=8)
                load(U_SSD + 1,
                     [(both[:, :, P * j:P * j + P],
                       w_in_mix[0][:, bass.ds(col + P * g, P)].rearrange("(k p) n -> p k n", p=P))
                      for j, col in enumerate((COL_B, COL_C))], g, 3)
                col_unit(U_SSD + 2, w_in_mix[0], COL_Z + 256 * g, g, 3)
            for u in range(4):
                col_unit(U_GA + u, w_in_mix[0], COL_GA + 256 * u)
            for u in range(4):
                row_unit(U_PA + u, proj_a[0], 256 * u)
            for u in range(8):
                row_unit(U_PB + u, proj_b[0], 256 * u)
            for u in range(4):
                col_unit(U_GB + u, w_in_mix[0], COL_GB + 256 * u)
            for u in range(4):
                row_unit(U_WO + u, w_out_mix[0], 256 * u)
            ffn(1, U_F2IN, U_F2OUT)
            for b in range(4):
                sp.wait_ge(out_copied, b + 1)
                sp.dma_start(out[0, :, 256 * b:256 * b + 256].rearrange("(s p) d -> p s d", p=P),
                             out_tok[:, b]).then_inc(stored, 16)
            sp.wait_ge(stored, 4 * 16)

        @block.gpsimd
        def _(pool):
            pool.memset(eps[:], EPS).then_inc(ones_set, 1)
            pool.memset(ones[:], 1.0).then_inc(ones_set, 1)
            pool.memset(ones_d[:], 1.0 / D).then_inc(ones_set, 1)
            pool.memset(ones_g[:], HG ** -1 * HP ** -1).then_inc(ones_set, 1)

            def ada_src(chunk, k2):
                return w_ada[0][k2 * 256:(k2 + 1) * 256, bass.ds(chunk * D, D)].rearrange("(k p) n -> p k n", p=P)

            for j in range(8):
                if j >= 4:
                    pool.wait_ge(ada_used, j - 3)
                dst = ada_ring[:, j % 4, :] if j % 4 < 2 else scratch[:, (j % 4 - 2) * 2048:(j % 4 - 1) * 2048]
                pool.dma_start(dst.rearrange("p (k n) -> p k n", k=2), ada_src((SC1, SH1)[j // 4], j % 4)).then_inc(
                    ada_loaded[j % 4], 16)

            def ada_loads(first, end):
                with pool.Fori(first, end) as ch:
                    for j in range(4):
                        pool.wait_ge(ada_used, 4 * ch + j - 1)
                        pool.dma_start(ada_ring[:, j % 2, :].rearrange("p (k n) -> p k n", k=2),
                                       ada_src(ch, j)).then_inc(ada_loaded[j % 2], 16)

            def add_part(f):
                for b in range(4):
                    pool.wait_ge(term_ready, KT * f + 2 * b + 2)
                    pool.tensor_tensor(hT[:, 2 * b:2 * b + 2, :], hT[:, 2 * b:2 * b + 2, :],
                                       work[:, 2 * b:2 * b + 2, :], ALU.add).then_inc(h_ready, 1)

            ada_loads(G1, SH2)
            add_part(0)
            pool.wait_ge(const_loaded, 16)
            pool.wait_ge(dt_done, 1)
            pool.tensor_copy(sel, ident[0:SH, 0:HG].unsqueeze(2).to_broadcast([SH, HG, P])).then_inc(sel_ready, 1)
            with pool.Fori(1, G) as g:
                pool.wait_ge(ssd_cum, g)
                pool.tensor_copy(sel, ident[0:SH, bass.ds(HG * g, HG)].unsqueeze(2).to_broadcast([SH, HG, P])
                                 ).then_inc(sel_ready, 1)
            ada_loads(SH2, MODS)
            add_part(1)
            add_part(2)

        @block.scalar
        def _(act):
            def split(n, i=0, step=0, halves=(0, 1)):
                if n >= UNITS:
                    return
                act.wait_ge(raw_loaded[n % RAW], 32 * (n // RAW + 1) + 32 * (step // RAW) * i)
                for g in halves:
                    if 2 * n + g >= GR:
                        act.wait_ge(used, split_count(n, g, i, step) - GR)
                    nc.scalar.activation(w_high[:, granule(n, g), :], raw[:, n % RAW, g * 1024:(g + 1) * 1024],
                                         ACT.Copy).then_inc(high_ready, 1)

            act.dma_start(rel_tab[:], rel_bias).then_inc(onehot_loaded, 16)
            act.dma_start(onehot, k_onehot).then_inc(onehot_loaded, 16)
            act.dma_start(causal, k_causal).then_inc(onehot_loaded, 16)

            act.wait_ge(c_turned, 1)
            nc.scalar.activation(cs[:], ps[:, 4, 0:KT], ACT.Silu).then_inc(cs_ready, 1)
            for b in range(4):
                act.wait_ge(x_turned, b + 1)
                nc.scalar.activation(hT[:, 2 * b:2 * b + 2, :], ps[:, b, :].rearrange("p (k t) -> p k t", k=2),
                                     ACT.Copy).then_inc(x_copied, 1)
            for b in range(4):
                act.wait_ge(x_copied, 4)
                act.wait_ge(x_turned, 4)
                nc.scalar.activation(work[:, 2 * b:2 * b + 2, :], hT[:, 2 * b:2 * b + 2, :],
                                     ACT.Square).then_inc(squared, 1)

            def root_table():
                nc.scalar.preload_act_table(ACT.Sqrt)

            def root(m, bank):
                act.wait_ge(mean_done, m + 1)
                nc.scalar.activation(rms[:], ps[:, bank, 0:T], ACT.Sqrt, bias=eps[:]).then_inc(root_ready, 1)

            def shift(f):
                if f == 0:
                    act.wait_ge(mod_ready, 2)
                for k in range(KT):
                    act.wait_ge(scaled, KT * f + k + 1)
                    nc.scalar.activation(u_high[:, k, :], work[:, k, :], ACT.Identity,
                                         bias=mod[:, 3 * f, k:k + 1]).then_inc(u_hi, 1)

            def after_part(f, bank, last=False):
                for b in range(4):
                    if b < 3:
                        act.wait_ge(part_done, 3 * f + b + 1)
                    else:
                        act.wait_ge(used, 2 * (U_QKV, U_F2IN, UNITS)[f])
                    nc.scalar.activation(work[:, 2 * b:2 * b + 2, :],
                                         ps[:, bank + b, :].rearrange("p (k t) -> p k t", k=2),
                                         ACT.Square).then_inc(squared, 1)
                split((U_QKV, U_F2IN, UNITS)[f] + 2, halves=(1,))
                root(2 * f + 1, 0)
                if last:
                    return
                for b in range(4):
                    act.wait_ge(h_ready, 4 * f + b + 1)
                    nc.scalar.activation(work[:, 2 * b:2 * b + 2, :], hT[:, 2 * b:2 * b + 2, :],
                                         ACT.Square).then_inc(squared, 1)
                root(2 * f + 2, 1)

            def ffn(f, u_in, u_out):
                def pair(p, i=0):
                    n = u_in + 2 * p
                    split(n + 3, i, 6)
                    split(n + 4, i, 6)
                    act.wait_ge(used, 2 * n + 4 + 12 * i)
                    if f == 0 and p == 0:
                        act.wait_ge(par_turned, 3)
                    nc.scalar.activation(silu_a[:, p % 3, :], ps[:, 2 * (p % 3), :], ACT.Silu).then_inc(silu_done, 1)
                    act.wait_ge(s_done, PAIRS * f + p + 1 + 3 * i)
                    nc.scalar.activation(in_high[:, bass.ds(2 * p + 6 * i, 2), :],
                                         silu_a[:, p % 3, :].rearrange("p (k t) -> p k t", k=2),
                                         ACT.Copy).then_inc(s_hi, 1)

                pair(0)
                if f == 0:
                    act.wait_ge(toep_turned, 1)
                    for b in range(4):
                        nc.scalar.activation(toep[:, 2 * b:2 * b + 2, :],
                                             ps[:, 4 + b, :].rearrange("p (h k) -> p h k", h=2),
                                             ACT.Copy).then_inc(toep_ready, 1)
                pair(1)
                with act.Fori(0, (PAIRS - 2) // 3) as i:
                    for p in range(2, 5):
                        pair(p, i)
                root_table()
                if f == 0:
                    with act.Fori(0, PAIRS // 3) as i:
                        for u in range(3):
                            split(u_out + u + 3, i, 3)
                    for u in range(PAIRS // 3 * 3, PAIRS - 1):
                        split(u_out + u + 3)
                    split(u_out + PAIRS + 2, halves=(0,))
                else:
                    with act.Fori(0, (PAIRS - 3) // 3) as i:
                        for u in range(3):
                            split(u_out + u + 3, i, 3)
                    for u in range((PAIRS - 3) // 3 * 3, PAIRS):
                        split(u_out + u + 3)

            def dt_chain():
                act.wait_ge(dt_in, 1)
                nc.scalar.activation(dts[:, 1], dts[:, 0], ACT.Abs).then_inc(dt_act, 1)
                act.wait_ge(dt_act, 1)
                nc.scalar.activation(dts[:, 2], dts[:, 1], ACT.Exp, scale=-1.0).then_inc(dt_act, 1)
                nc.scalar.activation(aexp[:], aexp[:], ACT.Exp).then_inc(dt_act, 1)
                act.wait_ge(dt_act, 3)
                nc.scalar.activation(dts[:, 3], dts[:, 2], ACT.Ln, bias=1.0).then_inc(dt_act, 1)

            def turn_copy(i):
                act.wait_ge(probs_turned, i + 1)
                nc.scalar.activation(probsT, ps[:, 5:7, 0:384], ACT.Copy).then_inc(probsT_ready, 1)

            def o_split(i):
                act.wait_ge(pv_done, i + 1)
                nc.scalar.activation(in_high[:, bass.ds(2 * i, 2), :],
                                     ps[:, 7, :].rearrange("p (h q) -> p h q", h=2), ACT.Copy).then_inc(o_hi, 1)

            def attention(i, first):
                if first:
                    n, r = U_QKV, 0
                else:
                    n, r = U_QKV, i
                split(n + 3, r, 3)
                act.wait_ge(used, 2 * n + 2 + 6 * r)
                nc.scalar.activation(qT, ps[:, 0, :].rearrange("p (h q) -> p h q", h=2), ACT.Copy,
                                     scale=float(P) ** -0.5).then_inc(q_copied, 1)
                if first:
                    dt_chain()
                split(n + 4, r, 3)
                if not first:
                    turn_copy(i - 1)
                split(n + 5, r, 3)
                act.wait_ge(used, 2 * n + 6 + 6 * r)
                nc.scalar.activation(vT, ps[:, 2, :].rearrange("p (h q) -> p h q", h=2),
                                     ACT.Copy).then_inc(v_copied, 1)
                if first:
                    act.wait_ge(cum_turned, 1)
                    nc.scalar.activation(cum_high[:], ps[0:SH, 6, 0:T], ACT.Copy).then_inc(cum_hi, 1)
                else:
                    o_split(i - 1)
                act.wait_ge(max_ready, i + 1)
                for j in range(4):
                    part = probs[:, j % 2, 0:256] if j < 2 else probs[:, j % 2, 256:384]
                    ins = nc.scalar.activation(part, part, ACT.Exp, bias=nmax[:, j:j + 1],
                                               accum_out=rsum[:, j:j + 1])
                ins.then_inc(exp_done, 1)

            def decays(g):
                act.wait_ge(ssd_cum, g + 1)
                for j in range(HG):
                    run = ps[:, 5 + j // 2, 256 * (j % 2):256 * (j % 2) + 256]
                    nc.scalar.activation(decay[:, j, 0:256], run, ACT.Relu, scale=-1.0,
                                         bias=cum[:, 0, bass.ds(HG * g + j, 1)])
                    ins = nc.scalar.activation(decay[:, j, 256:384], run[:, 128:256], ACT.Relu, scale=-1.0,
                                               bias=cum[:, 1, bass.ds(HG * g + j, 1)])
                ins.then_inc(seg_done, 1)
                act.wait_ge(seg_done, g + 1)
                nc.scalar.activation(decay, decay, ACT.Exp, scale=-1.0).then_inc(decay_ready, 1)

            def tap(bank, j, tile):
                nc.scalar.activation(conv[:, j, :], ps[:, bank, 256 * (j % 2):256 * (j % 2) + 256], ACT.Identity,
                                     scale=par2[:, TAPS - 1, tile], bias=par3[:, tile]).then_inc(tap_done, 1)

            def z_gate(g):
                nc.scalar.activation(ssm_z, ps[:, 2, :], ACT.Silu).then_inc(z_silu, 1)

            def g_square(g):
                act.wait_ge(y_gated, g + 1)
                nc.scalar.activation(gsq, yg, ACT.Square).then_inc(g_squared, 1)

            def g_sqrt(g):
                act.wait_ge(g_mean, g + 1)
                nc.scalar.activation(rms_g, ps[:, 3, 0:T], ACT.Sqrt, bias=eps[:]).then_inc(g_root, 1)

            def g_split(g):
                act.wait_ge(g_normed, g + 1)
                nc.scalar.activation(in_high[:, bass.ds(8 + 2 * g, 2), :], yg, ACT.Copy).then_inc(g_hi, 1)

            def ssm(g, first):
                n, r = U_SSD, (0 if first else g)
                if first:
                    turn_copy(H // 2 - 1)
                else:
                    decays(g - 1)
                split(n + 3, r, 3)
                act.wait_ge(used, 2 * n + 2 + 6 * r)
                if first:
                    act.wait_ge(probs_ready, H // 2)
                else:
                    act.wait_ge(skip_ready, g)
                tap(0, 0, bass.ds(2 * g, 1))
                tap(0, 1, bass.ds(2 * g + 1, 1))
                if not first:
                    z_gate(g - 1)
                act.wait_ge(conv_done, 2 * g + 1)
                nc.scalar.activation(conv[:, 0:2, :], conv[:, 0:2, :], ACT.Silu).then_inc(conv_silu, 1)
                split(n + 4, r, 3)
                if first:
                    o_split(H // 2 - 1)
                else:
                    g_square(g - 1)
                act.wait_ge(used, 2 * n + 4 + 6 * r)
                tap(1, 2, bass.ds(16 + g, 1))
                tap(1, 3, bass.ds(24 + g, 1))
                act.wait_ge(conv_done, 2 * g + 2)
                nc.scalar.activation(conv[:, 2:4, :], conv[:, 2:4, :], ACT.Silu).then_inc(conv_silu, 1)
                if not first:
                    g_sqrt(g - 1)
                    g_split(g - 1)
                split(n + 5, r, 3)
                act.wait_ge(used, 2 * n + 6 + 6 * r)

            root_table()
            root(0, 6)
            act.wait_ge(bias_copied, 1)
            act.dma_start(bias_rows, causal).then_inc(bias_stored, 16)
            split(0)
            shift(0)
            split(1)
            split(2)
            act.wait_ge(small_loaded, 10 * 16)
            nc.scalar.activation(dtw_high, dtw[:], ACT.Copy).then_inc(dtw_hi, 1)
            act.wait_ge(bias_stored, 16)
            act.wait_ge(ada_used, 8)
            act.dma_start(hankel, bass.AP(bias_rows.tensor, 0, [[1, P], [384, H], [1, T]])).then_inc(hankel_loaded, 16)

            ffn(0, U_F1IN, U_F1OUT)
            after_part(0, 4)
            shift(1)
            attention(0, True)
            with act.Fori(1, H // 2) as i:
                attention(i, False)
            ssm(0, True)
            with act.Fori(1, G) as g:
                ssm(g, False)
            decays(G - 1)
            z_gate(G - 1)
            for u in range(4):
                split(U_GA + u + 3)
                if u == 1:
                    g_square(G - 1)
                if u == 2:
                    g_sqrt(G - 1)
                    g_split(G - 1)
                act.wait_ge(used, 2 * (U_GA + u) + 2)
                nc.scalar.activation(work[:, 2 * u:2 * u + 2, :],
                                     ps[:, GA_BANK[u], :].rearrange("p (k t) -> p k t", k=2),
                                     ACT.Sigmoid).then_inc(gate_a_done, 1)
            for n in range(U_PA, U_GB):
                split(n + 3)
            for u in range(4):
                split(U_GB + u + 3)
                act.wait_ge(used, 2 * (U_GB + u) + 2)
                if u >= 2:
                    act.wait_ge(gate_b_used, u - 1)
                nc.scalar.activation(gate_b[:, u % 2, :], ps[:, u % 2, :], ACT.Sigmoid).then_inc(gate_b_done, 1)
                act.wait_ge(mixed_b, u + 1)
                nc.scalar.activation(in_high[:, 2 * u:2 * u + 2, :], work[:, 2 * u:2 * u + 2, :],
                                     ACT.Copy).then_inc(m_hi, 1)
            for n in range(U_WO, U_F2IN - 1):
                split(n + 3)
            root_table()
            split(U_F2IN + 2, halves=(0,))
            after_part(1, 2)
            shift(2)
            ffn(1, U_F2IN, U_F2OUT)
            after_part(2, 4, last=True)
            for b in range(4):
                act.wait_ge(out_turned, b + 1)
                nc.scalar.activation(out_tok[:, b], ps[:, b, :].rearrange("p (s d) -> p s d", s=2),
                                     ACT.Copy).then_inc(out_copied, 1)

        @block.vector
        def _(dve):
            step = [0]

            def after(ins):
                step[0] += 1
                ins.then_inc(own, 1)
                dve.wait_ge(own, step[0])

            def split(n, i=0, step=0, halves=(0, 1)):
                if n >= UNITS:
                    return
                for g in halves:
                    dve.wait_ge(high_ready, split_count(n, g, i, step))
                    dve.tensor_tensor(w_low[:, granule(n, g), :], raw[:, n % RAW, g * 1024:(g + 1) * 1024],
                                      w_high[:, granule(n, g), :].bitcast(F32), ALU.subtract).then_inc(low_ready, 1)

            def ada_unit(ch, j, i=0):
                acc = ada_acc1 if ch == 1 else ada_acc[:]
                if ch < 2:
                    slot, count = j, 16 * (ch + 1)
                else:
                    slot = j % 2
                    count = 16 * (2 + 2 * (ch - 2) + j // 2 + 1) + 32 * i
                src = ada_ring[:, slot, :] if slot < 2 else scratch[:, (slot - 2) * 2048:(slot - 1) * 2048]
                dve.wait_ge(ada_loaded[slot], count)
                if j == 0 and ch >= 2:
                    dve.wait_ge(ada_summed, ch + i)
                for k in range(2):
                    part, col = src[:, k * D:(k + 1) * D], cs[:, 2 * j + k:2 * j + k + 1]
                    if j == 0 and k == 0:
                        ins = dve.tensor_scalar(acc, part, col, None, ALU.mult)
                    else:
                        dve.wait_ge(ada_step, 8 * ch + 2 * j + k + 8 * i)
                        ins = dve.scalar_tensor_tensor(out=acc, in0=part, scalar=col, in1=acc,
                                                       op0=ALU.mult, op1=ALU.add)
                    ins.then_inc(ada_step, 1)
                dve.wait_ge(ada_step, 8 * ch + 2 * j + 2 + 8 * i)
                dve.sem_inc(ada_used, 1)
                if j == 3:
                    dve.sem_inc(ada_ready, 1)

            def ada_take(ch, bank, i=0, nth=None):
                dve.wait_ge(ada_summed, (ch if nth is None else nth) + 1 + i)
                dve.tensor_tensor(mod[:, bass.ds(ch + i, 1), :].rearrange("p a k -> p (a k)"), ps[:, bank, 0:KT],
                                  par1[:, bass.ds(KT + KT * ch + KT * i, KT)], ALU.add).then_inc(mod_ready, 1)

            def gain(m):
                return par1[:, 80 + 8 * m:88 + 8 * m]

            def make_scale_in(f):
                dve.wait_ge(mod_ready, 3 * f + 2 if f else 1)
                after(dve.scalar_tensor_tensor(out=scale_in[:, f, :], in0=mod[:, 3 * f + 1, :], scalar=1.0,
                                               in1=gain(2 * f), op0=ALU.add, op1=ALU.mult))

            def make_scale_out(f):
                dve.wait_ge(mod_ready, 3 * f + 3)
                after(dve.scalar_tensor_tensor(out=scale_out[:, f, :], in0=mod[:, 3 * f + 2, :],
                                               scalar=1.0 if f == 1 else 0.5, in1=gain(2 * f + 1),
                                               op0=ALU.mult, op1=ALU.mult))

            def make_rms(m):
                dve.wait_ge(root_ready, m + 1)
                dve.reciprocal(rms[:], rms[:]).then_inc(rms_ready, 1)
                dve.wait_ge(rms_ready, m + 1)

            def in_norm(f):
                make_rms(2 * f)

                def low(k):
                    dve.wait_ge(u_hi, KT * f + k + 1)
                    dve.scalar_tensor_tensor(out=u_low[:, k, :], in0=work[:, k, :], scalar=mod[:, 3 * f, k:k + 1],
                                             in1=u_high[:, k, :].bitcast(F32), op0=ALU.add,
                                             op1=ALU.subtract).then_inc(u_lo, 1)

                for k in range(KT):
                    dve.scalar_tensor_tensor(out=work[:, k, :], in0=hT[:, k, :], scalar=scale_in[:, f, k:k + 1],
                                             in1=rms[:], op0=ALU.mult, op1=ALU.mult).then_inc(scaled, 1)
                    if f and k >= 2:
                        low(k - 2)
                if f:
                    low(KT - 2)
                    low(KT - 1)
                    return
                split(0, halves=(0,))
                ada_take(SH1, 7, nth=1)
                for k in range(KT):
                    low(k)
                    if k == 3:
                        split(0, halves=(1,))

            def scale_part(f, bank):
                make_rms(2 * f + 1)
                for k in range(KT):
                    dve.scalar_tensor_tensor(out=work[:, k, :],
                                             in0=ps[:, bank + k // 2, T * (k % 2):T * (k % 2) + T],
                                             scalar=scale_out[:, f, k:k + 1], in1=rms[:], op0=ALU.mult,
                                             op1=ALU.mult).then_inc(term_ready, 1)

            def ffn(f, u_in, u_out):
                def gate(p, i=0):
                    dve.wait_ge(silu_done, PAIRS * f + p + 1 + 3 * i)
                    dve.tensor_tensor(silu_a[:, p % 3, :], silu_a[:, p % 3, :], ps[:, 2 * (p % 3) + 1, :],
                                      ALU.mult).then_inc(s_done, 1)

                def low(p, i=0):
                    dve.wait_ge(s_hi, PAIRS * f + p + 1 + 3 * i)
                    dve.tensor_tensor(in_low[:, bass.ds(2 * p + 6 * i, 2), :],
                                      silu_a[:, p % 3, :].rearrange("p (k t) -> p k t", k=2),
                                      in_high[:, bass.ds(2 * p + 6 * i, 2), :].bitcast(F32),
                                      ALU.subtract).then_inc(s_lo, 1)

                for p in range(2):
                    split(u_in + 2 * p + 3)
                    split(u_in + 2 * p + 4)
                    gate(p)
                    if f == 0:
                        ada_unit(G1, 2 * p)
                        ada_unit(G1, 2 * p + 1)
                    low(p)
                with dve.Fori(0, (PAIRS - 2) // 3) as i:
                    for p in range(2, 5):
                        n = u_in + 2 * p
                        split(n + 3, i, 6)
                        split(n + 4, i, 6)
                        gate(p, i)
                        if f == 0 and p == 3:
                            ada_take(G1, 7, i)
                            ada_unit(SHM, 0, i)
                            ada_unit(SHM, 1, i)
                        if f == 0 and p == 4:
                            ada_unit(SHM, 2, i)
                            ada_unit(SHM, 3, i)
                        low(p, i)
                end = PAIRS // 3 * 3 if f == 0 else (PAIRS - 3) // 3 * 3
                with dve.Fori(0, end // 3) as i:
                    for u in range(3):
                        split(u_out + u + 3, i, 3)
                if f == 0:
                    ada_take(GM, 0)
                    make_scale_out(0)
                    make_scale_in(1)
                    make_scale_out(1)
                for u in range(end, PAIRS):
                    split(u_out + u + 3)

            def turn_copy(i):
                dve.wait_ge(probs_turned, i + 1)
                dve.tensor_copy(v_tok, ps[:, 7, :].rearrange("p (h s d) -> p h s d", h=2, s=2)).then_inc(v_ready, 1)

            def o_split(i):
                dve.wait_ge(o_hi, i + 1)
                dve.tensor_tensor(in_low[:, bass.ds(2 * i, 2), :], ps[:, 7, :].rearrange("p (h q) -> p h q", h=2),
                                  in_high[:, bass.ds(2 * i, 2), :].bitcast(F32), ALU.subtract).then_inc(o_lo, 1)

            def dt_chain():
                dve.wait_ge(dt_done, 1)
                dve.tensor_tensor(dts[:, 0], ps[:, 5, 0:2 * SH].rearrange("p (s h) -> p s h", s=2),
                                  dtb[:].unsqueeze(1).to_broadcast([P, 2, SH]), ALU.add).then_inc(dt_in, 1)
                dve.wait_ge(dt_in, 1)
                dve.wait_ge(dt_act, 4)
                after(dve.tensor_scalar(dts[:, 1], dts[:, 0], 0.0, None, ALU.max))
                after(dve.tensor_tensor(dt[:], dts[:, 1], dts[:, 3], ALU.add))
                dve.scalar_tensor_tensor(out=dts[:, 2], in0=dt[:], scalar=-1.0,
                                         in1=aexp[:].unsqueeze(1).to_broadcast([P, 2, SH]), op0=ALU.mult,
                                         op1=ALU.mult).then_inc(dt_ready, 1)

            def attention(i, first):
                n, r = U_QKV, (0 if first else i)
                split(n + 3, r, 3)
                if first:
                    dt_chain()
                split(n + 4, r, 3)
                dve.wait_ge(used, 2 * n + 4 + 6 * r)
                dve.tensor_copy(kTt, ps[:, 1, :].rearrange("p (h q) -> p h q", h=2)).then_inc(k_copied, 1)
                if not first:
                    turn_copy(i - 1)
                split(n + 5, r, 3)
                if first:
                    dve.wait_ge(cum_done, 1)
                    dve.tensor_copy(cum[:], ps[:, 5, 2 * SH:4 * SH].rearrange("p (s h) -> p s h", s=2)
                                    ).then_inc(cum_copied, 1)
                    dve.wait_ge(toep_ready, 4)
                dve.wait_ge(scores_done, i + 1)
                dve.tensor_tensor(probs[:, :, 0:256], ps[:, 3:5, 0:256], toep[:, bass.ds(2 * i, 2), :],
                                  ALU.add).then_inc(softmax_step, 1)
                dve.tensor_tensor(probs[:, :, 256:384], ps[:, 3:5, 256:384], toep[:, bass.ds(2 * i, 2), 128:256],
                                  ALU.add).then_inc(softmax_step, 1)
                dve.wait_ge(softmax_step, 7 * i + 2)
                dve.tensor_reduce(rsum[:, 0:2], probs[:, :, 0:256], AX_X, ALU.max).then_inc(softmax_step, 1)
                dve.tensor_reduce(rsum[:, 2:4], probs[:, :, 256:384], AX_X, ALU.max).then_inc(softmax_step, 1)
                dve.wait_ge(softmax_step, 7 * i + 4)
                dve.tensor_scalar(nmax[:], rsum[:], -1.0, None, ALU.mult).then_inc(max_ready, 1)
                if first:
                    dve.wait_ge(cum_hi, 1)
                    dve.tensor_tensor(cum_low[:], ps[0:SH, 6, 0:T], cum_high[:].bitcast(F32),
                                      ALU.subtract).then_inc(cum_lo, 1)
                else:
                    o_split(i - 1)
                dve.wait_ge(exp_done, i + 1)
                dve.reciprocal(rsum[:], rsum[:]).then_inc(softmax_step, 1)
                dve.wait_ge(softmax_step, 7 * i + 5)
                dve.tensor_tensor(probs[:, :, 0:256], probs[:, :, 0:256],
                                  rsum[:, 0:2].unsqueeze(2).to_broadcast([P, 2, 256]),
                                  ALU.mult).then_inc(softmax_step, 1)
                dve.tensor_tensor(probs[:, :, 256:384], probs[:, :, 256:384],
                                  rsum[:, 2:4].unsqueeze(2).to_broadcast([P, 2, 128]),
                                  ALU.mult).then_inc(softmax_step, 1)
                dve.wait_ge(softmax_step, 7 * i + 7)
                dve.sem_inc(probs_ready, 1)

            def weights(g):
                dve.wait_ge(decay_ready, g + 1)
                dve.wait_ge(cbm_ready, g + 1)
                dve.tensor_tensor(decay, decay, cbm.unsqueeze(1).to_broadcast([P, HG, 384]),
                                  ALU.mult).then_inc(w_ready, 1)

            def taps(bank, j0, tiles, half, g):
                for t in range(1, TAPS):
                    for j in range(2):
                        if t == 1:
                            dve.wait_ge(tap_done, 4 * g + j0 + 2)
                        else:
                            dve.wait_ge(taps_step, 12 * g + 6 * half + 2 * (t - 2) + j + 1)
                        dve.scalar_tensor_tensor(out=conv[:, j0 + j, t:T], in0=ps[:, bank, T * j:T * j + T - t],
                                                 scalar=par2[:, TAPS - 1 - t, tiles[j]],
                                                 in1=conv[:, j0 + j, t:T], op0=ALU.mult,
                                                 op1=ALU.add).then_inc(taps_step, 1)
                dve.wait_ge(taps_step, 12 * g + 6 * half + 6)
                dve.sem_inc(conv_done, 1)

            def y_take(g):
                dve.wait_ge(y_done, g + 1)
                dve.tensor_tensor(yg, yg, ps[:, 7, :].rearrange("p (c t) -> p c t", c=2), ALU.add).then_inc(y_skip, 1)
                dve.wait_ge(y_skip, g + 1)
                dve.wait_ge(z_silu, g + 1)
                dve.tensor_tensor(yg, yg, ssm_z.rearrange("p (c t) -> p c t", c=2), ALU.mult).then_inc(y_gated, 1)

            def g_norm(g):
                dve.wait_ge(g_root, g + 1)
                dve.reciprocal(rms_g, rms_g).then_inc(g_rms, 1)
                dve.wait_ge(g_rms, g + 1)
                for q in range(2):
                    ins = dve.scalar_tensor_tensor(out=yg[:, q, :], in0=yg[:, q, :],
                                                   scalar=par3[:, bass.ds(32 + 2 * g + q, 1)], in1=rms_g,
                                                   op0=ALU.mult, op1=ALU.mult)
                ins.then_inc(g_normed, 1)

            def g_split(g):
                dve.wait_ge(g_hi, g + 1)
                dve.tensor_tensor(in_low[:, bass.ds(8 + 2 * g, 2), :], yg,
                                  in_high[:, bass.ds(8 + 2 * g, 2), :].bitcast(F32), ALU.subtract).then_inc(g_lo, 1)

            def ssm(g, first):
                n, r = U_SSD, (0 if first else g)
                if first:
                    turn_copy(H // 2 - 1)
                else:
                    weights(g - 1)
                split(n + 3, r, 3)
                taps(0, 0, (bass.ds(2 * g, 1), bass.ds(2 * g + 1, 1)), 0, g)
                if not first:
                    y_take(g - 1)
                split(n + 4, r, 3)
                if first:
                    o_split(H // 2 - 1)
                taps(1, 2, (bass.ds(16 + g, 1), bass.ds(24 + g, 1)), 1, g)
                if not first:
                    g_norm(g - 1)
                    g_split(g - 1)
                split(n + 5, r, 3)
                dve.wait_ge(ssd_in, g + 1)
                dve.tensor_tensor(xdt, ps[:, 4, :].rearrange("p (s h d) -> p s h d", s=2, h=HG),
                                  dt[:, :, bass.ds(HG * g, HG)].unsqueeze(3).to_broadcast([P, 2, HG, HP]),
                                  ALU.mult).then_inc(xdt_ready, 1)
                dve.tensor_tensor(cbm, ps[:, 3, 0:384], mask[:], ALU.mult).then_inc(cbm_ready, 1)
                if not first:
                    dve.wait_ge(g_lo, g)
                for q in range(2):
                    ins = dve.tensor_scalar(yg[:, q, :], conv[:, q, :], dskip[:, bass.ds(2 * g + q, 1)], None,
                                            ALU.mult)
                ins.then_inc(skip_ready, 1)
                dve.wait_ge(skip_ready, g + 1)

            dve.wait_ge(cs_ready, 1)
            for j in range(4):
                ada_unit(0, j)
            dve.wait_ge(par_turned, 1)
            dve.tensor_copy(par1[:], ps[:, 4, 0:P]).then_inc(par_copied, 1)
            ada_unit(1, 0)
            ada_unit(1, 1)
            dve.wait_ge(bias_made, 1)
            dve.tensor_tensor(causal, causal, ps[0:H, 5, 0:384], ALU.add).then_inc(bias_copied, 1)
            dve.wait_ge(par_copied, 1)
            ada_take(SC1, 7, nth=0)
            make_scale_in(0)
            ada_unit(1, 2)
            ada_unit(1, 3)
            in_norm(0)
            split(1)
            dve.wait_ge(par_turned, 3)
            dve.tensor_copy(par2[:].rearrange("p t r -> p (t r)"), ps[:, 4, P:2 * P]).then_inc(par_copied, 1)
            dve.tensor_copy(par3[:], ps[:, 4, 2 * P:2 * P + 48]).then_inc(par_copied, 1)
            split(2)
            dve.wait_ge(dtw_hi, 1)
            dve.tensor_tensor(dtw_low, dtw[:], dtw_high.bitcast(F32), ALU.subtract).then_inc(dtw_lo, 1)
            ffn(0, U_F1IN, U_F1OUT)
            scale_part(0, 4)
            in_norm(1)
            attention(0, True)
            with dve.Fori(1, H // 2) as i:
                attention(i, False)
            ssm(0, True)
            with dve.Fori(1, G) as g:
                ssm(g, False)
            weights(G - 1)
            for u in range(4):
                split(U_GA + u + 3)
                if u == 0:
                    y_take(G - 1)
                if u == 2:
                    g_norm(G - 1)
                    g_split(G - 1)
            for u in range(4):
                split(U_PA + u + 3)
                ada_unit(SH2, u)
            for b in range(4):
                dve.wait_ge(used, 2 * U_PB)
                dve.tensor_tensor(work[:, 2 * b:2 * b + 2, :], work[:, 2 * b:2 * b + 2, :],
                                  ps[:, b, :].rearrange("p (k t) -> p k t", k=2), ALU.mult).then_inc(mixed_a, 1)
            for u in range(8):
                split(U_PB + u + 3)
                if u == 1:
                    ada_take(SH2, 0)
                if 1 <= u < 5:
                    ada_unit(SC2, u - 1)
                if u == 6:
                    ada_take(SC2, 0)
                    make_scale_in(2)
                if u >= 6:
                    ada_unit(G2, u - 6)

            def m_split(u):
                dve.wait_ge(m_hi, u + 1)
                dve.tensor_tensor(in_low[:, 2 * u:2 * u + 2, :], work[:, 2 * u:2 * u + 2, :],
                                  in_high[:, 2 * u:2 * u + 2, :].bitcast(F32), ALU.subtract).then_inc(m_lo, 1)

            for u in range(4):
                split(U_GB + u + 3)
                dve.wait_ge(gate_b_done, u + 1)
                dve.tensor_tensor(gate_b[:, u % 2, :], gate_b[:, u % 2, :], ps[:, 4 + u, :],
                                  ALU.mult).then_inc(gate_b_used, 1)
                dve.wait_ge(gate_b_used, u + 1)
                dve.tensor_tensor(work[:, 2 * u:2 * u + 2, :], work[:, 2 * u:2 * u + 2, :],
                                  gate_b[:, u % 2, :].rearrange("p (k t) -> p k t", k=2),
                                  ALU.add).then_inc(mixed_b, 1)
                dve.wait_ge(mixed_b, u + 1)
                if u < 2:
                    ada_unit(G2, u + 2)
                m_split(u)
            ada_take(G2, 1)
            make_scale_out(2)
            for n in range(U_WO, U_F2IN):
                split(n + 3)
            scale_part(1, 2)
            in_norm(2)
            ffn(1, U_F2IN, U_F2OUT)
            scale_part(2, 4)

        @block.tensor
        def _(pe):
            def three(out, k_high, k_low, x_high, x_low, start, stop):
                pe.matmul(out, k_high, x_high, start=start, stop=False, skip_group_check=True)
                pe.matmul(out, k_high, x_low, start=False, stop=False, skip_group_check=True)
                return pe.matmul(out, k_low, x_high, start=False, stop=stop, skip_group_check=True)

            def col_unit(n, bank, i=0, step=0, fresh=None):
                for g in range(2):
                    pe.wait_ge(low_ready, split_count(n, g, i, step))
                    wh = w_high[:, granule(n, g), :].rearrange("p (k n) -> p k n", k=4)
                    wl = w_low[:, granule(n, g), :].rearrange("p (k n) -> p k n", k=4)
                    for k in range(4):
                        kt = 4 * g + k
                        if fresh is not None:
                            pe.wait_ge(u_lo, fresh + kt + 1)
                        for c2 in range(2):
                            ins = three(ps[:, bank, T * c2:T * c2 + T], wh[:, k, P * c2:P * c2 + P],
                                        wl[:, k, P * c2:P * c2 + P], u_high[:, kt, :], u_low[:, kt, :],
                                        kt == 0 and c2 == 0, kt == KT - 1)
                    ins.then_inc(used, 1)

            def row_unit(n, bank, kt, first, last, i=0, step=0, norm=None):
                for g in range(2):
                    pe.wait_ge(low_ready, split_count(n, g, i, step))
                    for m in range(8):
                        at = slice(P * m, P * m + P)
                        ins = three(ps[:, bank + m // 2, T * (m % 2):T * (m % 2) + T],
                                    w_high[:, granule(n, g), at], w_low[:, granule(n, g), at],
                                    in_high[:, bass.ds(kt + g, 1), :].rearrange("p a t -> p (a t)"),
                                    in_low[:, bass.ds(kt + g, 1), :].rearrange("p a t -> p (a t)"),
                                    first and g == 0 and m % 2 == 0, last and g == 1)
                        if norm is not None and g == 1 and m in (1, 3, 5):
                            ins.then_inc(part_done, 1)
                        if norm is not None and g == 1 and m in (3, 5):
                            mean_part(2 * norm + 1, 0, m // 2 - 1)
                    ins.then_inc(used, 1)

            def mean_part(m, bank, b):
                pe.wait_ge(squared, 4 * m + b + 1)
                for k in (2 * b, 2 * b + 1):
                    ins = pe.matmul(ps[:, bank, 0:T], ones_d[:], work[:, k, :], start=(k == 0), stop=(k == KT - 1),
                                    skip_group_check=True)
                if b == 3:
                    ins.then_inc(mean_done, 1)

            def mean(m, bank, first=0):
                for b in range(first, 4):
                    mean_part(m, bank, b)

            def ada_sum(ch, bank, i=0):
                acc = ada_acc1 if ch == 1 else ada_acc[:]
                pe.wait_ge(ada_ready, ch + 1 + i)
                for k in range(KT):
                    ins = pe.matmul(ps[:, bank, k:k + 1], acc[:, P * k:P * k + P], ones[:, 0:1],
                                    start=True, stop=True)
                ins.then_inc(ada_summed, 1)

            def ffn(f, u_in, u_out):
                def pair(p, i=0):
                    if p >= 2:
                        pe.wait_ge(s_done, PAIRS * f + p - 1 + 3 * i)
                    col_unit(u_in + 2 * p, 2 * (p % 3), i, 6, KT * (0, 2)[f] if p == 0 else None)
                    if f == 0 and p == 0:
                        pe.wait_ge(small_loaded, 10 * 16)
                        pe.transpose(ps[:, 4, P:2 * P], par[:, 1, :], ident[:]).then_inc(par_turned, 1)
                        pe.transpose(ps[:, 4, 2 * P:2 * P + 48], par[0:48, 2, :], ident[0:48, 0:48]).then_inc(par_turned, 1)
                    col_unit(u_in + 2 * p + 1, 2 * (p % 3) + 1, i, 6)

                def out_unit(u, i=0):
                    pe.wait_ge(s_lo, PAIRS * f + u + 1 + 3 * i)
                    row_unit(u_out + u, 4, 2 * u + 6 * i, u == 0, u == PAIRS - 1, i, 3,
                             norm=(0, 2)[f] if u == PAIRS - 1 else None)

                pair(0)
                if f == 0:
                    pe.wait_ge(hankel_loaded, 16)
                    pe.wait_ge(mod_ready, SC1 + 1)
                    pe.wait_ge(par_copied, 3)
                    pe.wait_ge(bias_copied, 1)
                    for b in range(4):
                        ins = pe.matmul(ps[:, 4 + b, :], flip[:], hankel[:, 2 * b:2 * b + 2, :], start=True, stop=True)
                    ins.then_inc(toep_turned, 1)
                pair(1)
                if f == 0:
                    pe.wait_ge(toep_ready, 4)
                with pe.Fori(0, (PAIRS - 2) // 3) as i:
                    for p in range(2, 5):
                        pair(p, i)
                        if f == 0 and p == 2:
                            ada_sum(G1, 7, i)
                pe.wait_ge(s_done, PAIRS * f + PAIRS - 2)
                if f == 0:
                    pe.wait_ge(mod_ready, GM)
                out_unit(0)
                if f == 0:
                    pe.wait_ge(s_done, PAIRS - 1)
                    ada_sum(GM, 0)
                else:
                    pe.wait_ge(s_done, 2 * PAIRS)
                with pe.Fori(0, (PAIRS - 2) // 3) as i:
                    for u in range(1, 4):
                        out_unit(u, i)
                if f == 0:
                    pe.wait_ge(mod_ready, GM + 1)
                out_unit(PAIRS - 1)

            def scores(i):
                pe.wait_ge(q_copied, i + 1)
                pe.wait_ge(k_copied, i + 1)
                for h in range(2):
                    pe.matmul(ps[:, 3 + h, 0:256], qT[:, h, 128:256], kTt[:, h, :], start=True, stop=True)
                    ins = pe.matmul(ps[:, 3 + h, 256:384], qT[:, h, 0:128], kTt[:, h, 0:128], start=True, stop=True)
                ins.then_inc(scores_done, 1)

            def turn(i):
                pe.wait_ge(probs_ready, i + 1)
                pe.wait_ge(v_copied, i + 1)
                for h in range(2):
                    for b, src in enumerate((256, 0, 128)):
                        pe.transpose(ps[:, 5 + h, P * b:P * b + P], probs[:, h, src:src + P], ident[:])
                for h in range(2):
                    for s in range(2):
                        at = (2 * h + s) * P
                        ins = pe.transpose(ps[:, 7, at:at + P], vT[:, h, s * P:s * P + P], ident[:])
                ins.then_inc(probs_turned, 1)

            def values(i):
                pe.wait_ge(probsT_ready, i + 1)
                pe.wait_ge(v_ready, i + 1)
                for h in range(2):
                    pe.matmul(ps[:, 7, T * h + P:T * h + T], v_tok[:, h, 1, :], probsT[:, h, 256:384],
                              start=True, stop=False, skip_group_check=True)
                    ins = pe.matmul(ps[:, 7, T * h:T * h + T], v_tok[:, h, 0, :], probsT[:, h, 0:256],
                                    start=False, stop=True, skip_group_check=True)
                ins.then_inc(pv_done, 1)

            def attention(i, first):
                n, r = U_QKV, (0 if first else i)
                if not first:
                    pe.wait_ge(q_copied, i)
                col_unit(n, 0, r, 3, KT if first else None)
                if first:
                    pe.wait_ge(dtw_lo, 1)
                    for s in range(2):
                        for k in range(KT):
                            at = slice(s * P, s * P + P)
                            dst = ps[:, 5, SH * s:SH * s + SH]
                            pe.matmul(dst, u_high[:, k, at], dtw_high[:, k, :], start=(k == 0), stop=False,
                                      skip_group_check=True)
                            pe.matmul(dst, u_high[:, k, at], dtw_low[:, k, :], start=False, stop=False,
                                      skip_group_check=True)
                            ins = pe.matmul(dst, u_low[:, k, at], dtw_high[:, k, :], start=False, stop=(k == KT - 1),
                                            skip_group_check=True)
                    ins.then_inc(dt_done, 1)
                else:
                    pe.wait_ge(k_copied, i)
                col_unit(n + 1, 1, r, 3)
                if not first:
                    turn(i - 1)
                    pe.wait_ge(v_copied, i)
                col_unit(n + 2, 2, r, 3)
                if first:
                    pe.wait_ge(dt_ready, 1)
                    da = dts[:, 2]
                    pe.matmul(ps[:, 5, 2 * SH:3 * SH], mask[:, 0:P], da[:, 0, :], start=True, stop=True)
                    pe.matmul(ps[:, 5, 3 * SH:4 * SH], ones[:], da[:, 0, :], start=True, stop=False,
                              skip_group_check=True)
                    pe.matmul(ps[:, 5, 3 * SH:4 * SH], mask[:, 0:P], da[:, 1, :], start=False, stop=True,
                              skip_group_check=True).then_inc(cum_done, 1)
                scores(i)
                if first:
                    pe.wait_ge(cum_copied, 1)
                    pe.transpose(ps[0:SH, 6, 0:P], cum[:, 0, :], ident[:])
                    pe.transpose(ps[0:SH, 6, P:2 * P], cum[:, 1, :], ident[:]).then_inc(cum_turned, 1)
                else:
                    values(i - 1)

            def stage_in(g):
                pe.wait_ge(conv_silu, 2 * g + 2)
                for s in range(2):
                    for q in range(2):
                        at = 256 * s + P * q
                        pe.transpose(ps[:, 4, at:at + P], conv[:, q, s * P:s * P + P], ident[:])
                pe.matmul(ps[:, 3, 0:T], conv[:, 2, 0:P], conv[:, 3, :], start=True, stop=True)
                pe.matmul(ps[:, 3, T:T + P], conv[:, 2, P:T], conv[:, 3, P:T], start=True,
                          stop=True).then_inc(ssd_in, 1)
                pe.wait_ge(sel_ready, g + 1)
                for j in range(HG):
                    dst = ps[:, 5 + j // 2, T * (j % 2):T * (j % 2) + T]
                    pe.matmul(dst, sel[:, j, :], cum_high[:], start=True, stop=False, skip_group_check=True)
                    ins = pe.matmul(dst, sel[:, j, :], cum_low[:], start=False, stop=True, skip_group_check=True)
                ins.then_inc(ssd_cum, 1)

            def stage_y(g):
                pe.wait_ge(w_ready, g + 1)
                pe.wait_ge(xdt_ready, g + 1)
                for j in range(HG):
                    half, at = 64 * (j % 2), T * (j // 2)
                    pe.matmul(ps[half:half + HP, 7, at + P:at + T], xdt[:, 1, j, :], decay[:, j, T:384],
                              start=True, stop=False, skip_group_check=True)
                    ins = pe.matmul(ps[half:half + HP, 7, at:at + T], xdt[:, 0, j, :], decay[:, j, 0:T],
                                    start=False, stop=True, skip_group_check=True)
                ins.then_inc(y_done, 1)

            def stage_mean(g):
                pe.wait_ge(g_squared, g + 1)
                pe.wait_ge(cbm_ready, g + 1)
                for q in range(2):
                    ins = pe.matmul(ps[:, 3, 0:T], ones_g[:], gsq[:, q, :], start=(q == 0), stop=(q == 1))
                ins.then_inc(g_mean, 1)

            def ssm(g, first):
                n, r = U_SSD, (0 if first else g)
                if first:
                    pe.wait_ge(q_copied, H // 2)
                else:
                    pe.wait_ge(conv_done, 2 * g - 1)
                col_unit(n, 0, r, 3)
                if first:
                    turn(H // 2 - 1)
                    pe.wait_ge(k_copied, H // 2)
                else:
                    stage_y(g - 1)
                    pe.wait_ge(conv_done, 2 * g)
                col_unit(n + 1, 1, r, 3)
                if first:
                    values(H // 2 - 1)
                    pe.wait_ge(v_copied, H // 2)
                else:
                    stage_mean(g - 1)
                    pe.wait_ge(z_silu, g)
                col_unit(n + 2, 2, r, 3)
                if first:
                    pe.wait_ge(o_lo, H // 2)
                else:
                    pe.wait_ge(g_rms, g)
                    pe.wait_ge(xdt_ready, g)
                    pe.wait_ge(seg_done, g)
                    pe.wait_ge(y_skip, g)
                stage_in(g)

            pe.wait_ge(const_loaded, 16)
            pe.wait_ge(c_loaded, 16)
            pe.transpose(ps[:, 4, 0:KT], par[0:KT, 0, :], ident[0:KT, 0:KT]).then_inc(c_turned, 1)
            pe.wait_ge(x_loaded, 16)
            x_tok = work[:].rearrange("p k t -> p (k t)").rearrange("p (s d) -> p s d", s=2)
            for k in range(KT):
                for s in range(2):
                    at = T * (k % 2) + P * s
                    ins = pe.transpose(ps[:, k // 2, at:at + P], x_tok[:, s, k * P:k * P + P], ident[:])
                if k % 2 == 1:
                    ins.then_inc(x_turned, 1)
            pe.wait_ge(ones_set, 4)
            pe.wait_ge(onehot_loaded, 3 * 16)
            pe.matmul(ps[0:H, 5, 0:384], rel_tab[:], onehot, start=True, stop=True).then_inc(bias_made, 1)
            pe.wait_ge(par_loaded, 7 * 16)
            pe.wait_ge(cs_ready, 1)
            pe.transpose(ps[:, 4, 0:P], par[:, 0, :], ident[:]).then_inc(par_turned, 1)
            mean(0, 6)
            ada_sum(0, 7)
            pe.wait_ge(mod_ready, 1)
            ada_sum(1, 7)
            ffn(0, U_F1IN, U_F1OUT)
            mean(1, 0, 2)
            mean(2, 1)
            attention(0, True)
            with pe.Fori(1, H // 2) as i:
                attention(i, False)
            ssm(0, True)
            with pe.Fori(1, G) as g:
                ssm(g, False)
            for u in range(4):
                if u == 0:
                    pe.wait_ge(conv_done, 2 * G - 1)
                if u == 1:
                    pe.wait_ge(conv_done, 2 * G)
                if u == 2:
                    pe.wait_ge(z_silu, G)
                if u == 3:
                    pe.wait_ge(gate_a_done, 1)
                col_unit(U_GA + u, GA_BANK[u])
                if u == 0:
                    stage_y(G - 1)
                if u == 1:
                    stage_mean(G - 1)
            pe.wait_ge(gate_a_done, 4)
            pe.wait_ge(g_rms, G)
            for u in range(4):
                row_unit(U_PA + u, 0, 2 * u, u == 0, u == 3)
            pe.wait_ge(xdt_ready, G)
            pe.wait_ge(seg_done, G)
            pe.wait_ge(y_skip, G)
            for u in range(8):
                pe.wait_ge(g_lo, u + 1)
                row_unit(U_PB + u, 4, 8 + 2 * u, u == 0, u == 7)
                if u == 0:
                    pe.wait_ge(mixed_a, 4)
                    ada_sum(SH2, 0)
                if u == 5:
                    ada_sum(SC2, 0)
            for u in range(4):
                if u == 0:
                    pe.wait_ge(mod_ready, SC2 + 1)
                if u >= 2:
                    pe.wait_ge(gate_b_done, u - 1)
                col_unit(U_GB + u, u % 2)
            pe.wait_ge(gate_b_used, 2)
            for u in range(4):
                pe.wait_ge(m_lo, u + 1)
                row_unit(U_WO + u, 2, 2 * u, u == 0, u == 3, norm=1 if u == 3 else None)
                if u == 0:
                    pe.wait_ge(gate_b_done, 4)
                    ada_sum(G2, 1)
            mean(3, 0, 2)
            pe.wait_ge(mod_ready, MODS)
            mean(4, 1)
            ffn(1, U_F2IN, U_F2OUT)
            mean(5, 0, 2)
            pe.wait_ge(rms_ready, 6)
            for b in range(4):
                pe.wait_ge(h_ready, 8 + b + 1)
                for k in range(2):
                    for s in range(2):
                        ins = pe.transpose(ps[:, b, T * s + P * k:T * s + P * k + P],
                                           hT[:, 2 * b + k, s * P:s * P + P], ident[:])
                ins.then_inc(out_turned, 1)


_INS = ['x', 'c', 'w_ada', 'b_ada', 'ffn1_norm_pre', 'ffn1_w_in', 'ffn1_w_out', 'ffn1_norm_post', 'mix_norm_pre',
        'w_in_mix', 'rel_bias', 'conv_w', 'conv_b', 'dt_bias', 'a_log', 'd_skip', 'ssm_norm_w', 'proj_a', 'proj_b',
        'w_out_mix', 'mix_norm_post', 'ffn2_norm_pre', 'ffn2_w_in', 'ffn2_w_out', 'ffn2_norm_post']


def constants():
    m = np.arange(384)
    rel = (T - 1) - m
    dist = np.maximum(rel, 0)
    exact = BUCKETS // 2
    large = exact + (np.log(np.maximum(dist, 1) / exact) / np.log(128 / exact) * (BUCKETS - exact)).astype(np.int64)
    bucket = np.where(dist < exact, dist, np.minimum(large, BUCKETS - 1))
    upper = np.triu(np.ones((P, P), np.float32))
    return {
        'k_ident': np.eye(P, dtype=np.float32),
        'k_flip': np.eye(P, dtype=np.float32)[::-1].copy(),
        'k_mask': np.concatenate([upper, np.ones((P, P), np.float32), upper], axis=1),
        'k_onehot': (np.arange(BUCKETS)[:, None] == bucket[None, :]).astype(np.float32),
        'k_causal': np.broadcast_to(np.where(rel < 0, NEG, 0.0).astype(np.float32), (H, 384)).copy(),
    }


def kernel(**inputs):
    import concourse.bacc as bacc
    from concourse.bass_utils import run_bass_kernel_spmd

    nc = bacc.Bacc("TRN2", target_bir_lowering=False, num_devices=1)
    arrays = {name: np.ascontiguousarray(inputs[name]) for name in _INS}
    arrays.update(constants())
    a = {name: nc.dram_tensor(f"in_{name}", v.shape, mybir.dt.from_np(v.dtype), kind="ExternalInput").ap()
         for name, v in arrays.items()}
    out = nc.dram_tensor("out_0", (1, T, D), F32, kind="ExternalOutput").ap()
    bias_rows = nc.dram_tensor("bias_rows", (H, 384), F32, kind="Internal").ap()
    build(nc, a['x'], a['c'], a['w_ada'], a['b_ada'],
          [a[n] for n in ('ffn1_norm_pre', 'ffn1_norm_post', 'mix_norm_pre', 'mix_norm_post', 'ffn2_norm_pre',
                          'ffn2_norm_post')],
          [a['ffn1_w_in'][0], a['ffn2_w_in'][0]], [a['ffn1_w_out'][0], a['ffn2_w_out'][0]], a['w_in_mix'],
          a['rel_bias'], a['conv_w'], a['conv_b'], a['dt_bias'], a['a_log'], a['d_skip'], a['ssm_norm_w'],
          a['proj_a'], a['proj_b'], a['w_out_mix'], a['k_ident'], a['k_flip'], a['k_mask'], a['k_onehot'], a['k_causal'],
          bias_rows, out)
    r = run_bass_kernel_spmd(nc, [{f"in_{n}": v for n, v in arrays.items()}], core_ids=[0])
    return r.results[0]["out_0"]
```

```python
from contextlib import ExitStack

import numpy as np

import concourse.bass as bass
from concourse import mybir

ALU = mybir.AluOpType
ACT = mybir.ActivationFunctionType
F32 = mybir.dt.float32
F32R = mybir.dt.float32r
AX_X = mybir.AxisListType.X

P = 128
T = 256
D = 1024
KT = D // P
H = 8
HID = 2816
INNER = 2048
SH = 32
G = 8
HG = SH // G
HP = INNER // SH
TAPS = 4
BUCKETS = 32
EPS = 1e-6
NEG = -1e30
MODS = 9
COL_Q, COL_K, COL_V = 0, D, 2 * D
COL_Z = 3 * D
COL_X = COL_Z + INNER
COL_B = COL_X + INNER
COL_C = COL_B + G * P
COL_DT = COL_C + G * P
COL_GA = COL_DT + SH
COL_GB = COL_GA + D
SH1, SC1, G1, SHM, SCM, GM, SH2, SC2, G2 = range(MODS)

PAIRS = HID // (2 * P)
RAW = 3
GR = 2 * RAW
U_F1IN = 0
U_F1OUT = U_F1IN + 2 * PAIRS
U_QKV = U_F1OUT + PAIRS
U_SSD = U_QKV + 12
U_GA = U_SSD + 3 * G
U_PA = U_GA + 4
U_PB = U_PA + 4
U_GB = U_PB + 8
U_WO = U_GB + 4
U_F2IN = U_WO + 4
U_F2OUT = U_F2IN + 2 * PAIRS
UNITS = U_F2OUT + PAIRS


def build(nc, x, c, w_ada, b_ada, norms, ffn_in, ffn_out, w_in_mix, rel_bias, conv_w, conv_b,
          dt_bias, a_log, d_skip, ssm_norm_w, proj_a, proj_b, w_out_mix,
          k_ident, k_flip, k_mask, k_onehot, k_causal, bias_rows, out):
    with ExitStack() as ctx:
        def sb(name, shape, dt=F32):
            return ctx.enter_context(nc.sbuf_tensor(name, shape, dt))

        def sem(name):
            return ctx.enter_context(nc.semaphore(name))

        ps = ctx.enter_context(nc.psum_tensor("ps", [P, 8, 512], F32))

        raw = sb("raw", [P, RAW, 2048])
        w_high = sb("w_high", [P, GR, 1024], F32R)
        w_low = sb("w_low", [P, GR, 1024], F32R)
        u_high = sb("u_high", [P, KT, T], F32R)
        u_low = sb("u_low", [P, KT, T], F32R)
        in_high = sb("in_high", [P, 24, T], F32R)
        in_low = sb("in_low", [P, 24, T], F32R)
        hT = sb("hT", [P, KT, T])
        work = sb("work", [P, KT, T])
        ada_ring = sb("ada_ring", [P, 2, 2048])
        ada_acc = sb("ada_acc", [P, D])
        ada_acc1 = raw[:, 2, 0:D]
        ada_parts = raw[:, 1].rearrange("p (j n) -> p j n", j=2)
        scratch = sb("scratch", [P, 5632])
        ident = sb("ident", [P, P])
        flip = sb("flip", [P, P])
        mask = sb("mask", [P, 384])
        ones = sb("ones", [P, P])
        ones_d = sb("ones_d", [P, P])
        ones_g = sb("ones_g", [P, P])
        par1 = sb("par1", [P, P])
        par2 = sb("par2", [P, TAPS, 32])
        par3 = sb("par3", [P, 48])
        cs = sb("cs", [P, KT])
        mod = sb("mod", [P, MODS, KT])
        scale_in = sb("scale_in", [P, 3, KT])
        scale_out = sb("scale_out", [P, 3, KT])
        rms = sb("rms", [P, T])
        dtw = sb("dtw", [P, KT, SH])
        dtw_parts = sb("dtw_parts", [P, 2, KT, SH], F32R)
        dtw_high, dtw_low = dtw_parts[:, 0], dtw_parts[:, 1]
        dtb = sb("dtb", [P, SH])
        aexp = sb("aexp", [P, SH])
        dskip = sb("dskip", [P, INNER // P])
        dts = sb("dts", [P, 4, 2, SH])
        dt = sb("dt", [P, 2, SH])
        cum = sb("cum", [P, 2, SH])
        cum_high = sb("cum_high", [SH, T], F32R)
        cum_low = sb("cum_low", [SH, T], F32R)
        sel = dtw_parts[0:SH].rearrange("p a k h -> p (a k h)").rearrange("p (j n) -> p j n", j=HG)
        nmax = sb("nmax", [P, 4])
        rsum = sb("rsum", [P, 4])
        eps = sb("eps", [P, 1])
        rel_tab = sb("rel_tab", [BUCKETS, H])

        par = scratch[:, 4096:4480].rearrange("p (r n) -> p r n", r=3)
        onehot = scratch[0:BUCKETS, 4480:4864]
        causal = scratch[0:H, 4864:5248]
        silu_a = scratch[:, 4096:5632].rearrange("p (r n) -> p r n", r=3)
        toep = scratch[:, 0:2048].rearrange("p (h k) -> p h k", h=H)
        hankel = scratch[:, 2048:4096].rearrange("p (h k) -> p h k", h=H)
        qT = scratch[:, 2048:2560].rearrange("p (h q) -> p h q", h=2)
        kTt = scratch[:, 2560:3072].rearrange("p (h q) -> p h q", h=2)
        vT = scratch[:, 3072:3584].rearrange("p (h q) -> p h q", h=2)
        v_tok = scratch[:, 3584:4096].rearrange("p (h s d) -> p h s d", h=2, s=2)
        probs = scratch[:, 4096:4864].rearrange("p (h k) -> p h k", h=2)
        probsT = scratch[:, 4864:5632].rearrange("p (h k) -> p h k", h=2)
        conv = scratch[:, 0:1024].rearrange("p (c t) -> p c t", c=4)
        ssm_z = scratch[:, 1024:1536]
        yg = scratch[:, 1536:2048].rearrange("p (c t) -> p c t", c=2)
        decay = scratch[:, 2048:3584].rearrange("p (h t) -> p h t", h=HG)
        cbm = scratch[:, 3584:3968]
        xdt = scratch[:, 4096:4608].rearrange("p (s h d) -> p s h d", s=2, h=HG)
        gsq = scratch[:, 4608:5120].rearrange("p (c t) -> p c t", c=2)
        rms_g = scratch[:, 5120:5376]
        newton = scratch[:, 5376:5632]
        out_tok = scratch[:, 0:2048].rearrange("p (b s d) -> p b s d", b=4, s=2)
        ada_acc_sh2 = scratch[:, 0:1024]
        ada_acc_g2 = scratch[:, 1024:2048]
        gate_b = scratch[:, 0:1024].rearrange("p (r n) -> p r n", r=2)

        raw_loaded = [sem(f"raw_loaded{i}") for i in range(RAW)]
        high_ready, low_ready, used = sem("high_ready"), sem("low_ready"), sem("used")
        const_loaded, par_loaded, x_loaded = sem("const_loaded"), sem("par_loaded"), sem("x_loaded")
        c_loaded, c_turned, part_done = sem("c_loaded"), sem("c_turned"), sem("part_done")
        small_loaded, ones_set = sem("small_loaded"), sem("ones_set")
        onehot_loaded, bias_made, bias_copied, bias_stored, hankel_loaded, toep_turned, toep_ready = (
            sem("onehot_loaded"), sem("bias_made"), sem("bias_copied"), sem("bias_stored"),
            sem("hankel_loaded"), sem("toep_turned"), sem("toep_ready"))
        par_turned, par_copied, cs_ready = sem("par_turned"), sem("par_copied"), sem("cs_ready")
        x_turned, x_copied = sem("x_turned"), sem("x_copied")
        ada_loaded = [sem(f"ada_loaded{i}") for i in range(4)]
        ada_used, ada_ready, ada_summed, mod_ready = (
            sem("ada_used"), sem("ada_ready"), sem("ada_summed"), sem("mod_ready"))
        ada_step, ada_scaled, parts_summed = sem("ada_step"), sem("ada_scaled"), sem("parts_summed")
        squared, mean_done, root_ready, rms_ready = (
            sem("squared"), sem("mean_done"), sem("root_ready"), sem("rms_ready"))
        pair_early, pair_late, quad_early, quad_late = (
            sem("pair_early"), sem("pair_late"), sem("quad_early"), sem("quad_late"))
        term_ready, h_early, h_late = sem("term_ready"), sem("h_early"), sem("h_late")
        scaled, u_hi, u_lo = sem("scaled"), sem("u_hi"), sem("u_lo")
        silu_done, s_done, s_hi, s_lo = sem("silu_done"), sem("s_done"), sem("s_hi"), sem("s_lo")
        dtw_hi, dtw_lo, dt_done, dt_in, dt_act, dt_ready = (
            sem("dtw_hi"), sem("dtw_lo"), sem("dt_done"), sem("dt_in"), sem("dt_act"), sem("dt_ready"))
        cum_done, cum_copied, cum_turned, cum_hi, cum_lo = (
            sem("cum_done"), sem("cum_copied"), sem("cum_turned"), sem("cum_hi"), sem("cum_lo"))
        q_copied, k_copied, v_copied = sem("q_copied"), sem("k_copied"), sem("v_copied")
        scores_done, softmax_step, max_ready, exp_done, probs_ready = (
            sem("scores_done"), sem("softmax_step"), sem("max_ready"), sem("exp_done"), sem("probs_ready"))
        probs_turned, probsT_ready, v_ready, pv_done, o_hi, o_lo = (
            sem("probs_turned"), sem("probsT_ready"), sem("v_ready"), sem("pv_done"), sem("o_hi"), sem("o_lo"))
        sel_ready, own, skip_ready = sem("sel_ready"), sem("own"), sem("skip_ready")
        tap_done, taps_step, conv_done, conv_silu, z_silu = (
            sem("tap_done"), sem("taps_step"), sem("conv_done"), sem("conv_silu"), sem("z_silu"))
        ssd_in, ssd_cum, xdt_ready, cbm_ready, seg_done, decay_ready, w_ready = (
            sem("ssd_in"), sem("ssd_cum"), sem("xdt_ready"), sem("cbm_ready"), sem("seg_done"), sem("decay_ready"),
            sem("w_ready"))
        y_done, y_skip, y_gated, g_squared, g_mean, g_root, g_rms, g_normed, g_hi, g_lo = (
            sem("y_done"), sem("y_skip"), sem("y_gated"), sem("g_squared"), sem("g_mean"), sem("g_root"), sem("g_rms"),
            sem("g_normed"), sem("g_hi"), sem("g_lo"))
        g_log, g_newton, g_summed = sem("g_log"), sem("g_newton"), sem("g_summed")
        gate_a_done, mixed_a, gate_b_done, gate_b_used, mixed_b, m_hi, m_lo = (
            sem("gate_a_done"), sem("mixed_a"), sem("gate_b_done"), sem("gate_b_used"), sem("mixed_b"), sem("m_hi"),
            sem("m_lo"))
        out_turned, out_copied, stored = sem("out_turned"), sem("out_copied"), sem("stored")

        GA_BANK = (0, 1, 5, 6)
        block = ctx.enter_context(nc.Block())

        def granule(n, g):
            return (2 * n + g) % GR

        def split_count(n, g, i, step):
            return 2 * n + g + 1 + 2 * step * i

        @block.sync
        def _(sp):
            def load(n, parts, i=0, step=0):
                if n >= RAW:
                    sp.wait_ge(low_ready, 2 * (n - RAW) + 2 + 2 * step * i)
                for dst, src in parts:
                    sp.dma_start(dst, src).then_inc(raw_loaded[n % RAW], 16)

            def halves(n):
                return [raw[:, n % RAW, g * 1024:(g + 1) * 1024] for g in range(2)]

            def col_unit(n, w, at, i=0, step=0):
                load(n, [(dst.rearrange("p (k n) -> p k n", k=4),
                          w[512 * g:512 * g + 512, bass.ds(at, 256)].rearrange("(k p) n -> p k n", p=P))
                         for g, dst in enumerate(halves(n))], i, step)

            def row_unit(n, w, at, i=0, step=0):
                load(n, [(dst, w[bass.ds(at + P * g, P), :]) for g, dst in enumerate(halves(n))], i, step)

            with nc.allow_non_contiguous_dma(reason="small"):
                sp.dma_start(ident[:], k_ident).then_inc(const_loaded, 16)
                sp.dma_start(par[0:8, 0, :], c.rearrange("a (r n) -> (a r) n", n=P)).then_inc(c_loaded, 16)
                sp.dma_start(work[:].rearrange("p k t -> p (k t)").rearrange("p (s d) -> p s d", s=2),
                             x[0].rearrange("(s p) d -> p s d", p=P)).then_inc(x_loaded, 16)
                sp.dma_start(par[8:80, 0, :], b_ada.rearrange("a (r n) -> (a r) n", n=P)).then_inc(par_loaded, 16)
                for m, g in enumerate(norms):
                    sp.dma_start(par[80 + 8 * m:88 + 8 * m, 0, :],
                                 g.rearrange("a (r n) -> (a r) n", n=P)).then_inc(par_loaded, 16)
            sp.wait_ge(ada_used, 5)

            def small_loads():
                with nc.allow_non_contiguous_dma(reason="small"):
                    for dst, src in (
                            (par[:, 1, :], conv_w[0].rearrange("t (r n) -> (t r) n", n=P)),
                            (par[0:32, 2, :], conv_b.rearrange("a (r n) -> (a r) n", n=P)),
                            (par[32:48, 2, :], ssm_norm_w.rearrange("a (r n) -> (a r) n", n=P)),
                            (flip[:], k_flip),
                            (mask[:], k_mask),
                            (dtw[:], w_in_mix[0][:, COL_DT:COL_DT + SH].rearrange("(k p) n -> p k n", p=P)),
                            (dtb[:], dt_bias.partition_broadcast(P)),
                            (aexp[:], a_log.partition_broadcast(P)),
                            (dskip[0:HP, :], d_skip[0].rearrange("(r s) -> s r", s=2)[0:1, :].partition_broadcast(HP)),
                            (dskip[HP:P, :], d_skip[0].rearrange("(r s) -> s r", s=2)[1:2, :].partition_broadcast(HP))):
                        sp.dma_start(dst, src).then_inc(small_loaded, 16)

            def ffn(f, u_in, u_out):
                w_in, w_out = ffn_in[f], ffn_out[f]

                def pair(p, i=0):
                    col_unit(u_in + 2 * p, w_in, 256 * p + 768 * i, i, 6)
                    if f == 0 and p == 0:
                        small_loads()
                        sp.wait_ge(parts_summed, 1)
                    col_unit(u_in + 2 * p + 1, w_in, HID + 256 * p + 768 * i, i, 6)

                pair(0)
                if f == 0:
                    sp.wait_ge(ada_summed, 2)
                pair(1)
                with sp.Fori(0, (PAIRS - 2) // 3) as i:
                    for p in range(2, 5):
                        pair(p, i)
                with sp.Fori(0, PAIRS // 3) as i:
                    for u in range(3):
                        row_unit(u_out + u, w_out, 256 * u + 768 * i, i, 3)
                for u in range(PAIRS // 3 * 3, PAIRS):
                    row_unit(u_out + u, w_out, 256 * u)

            ffn(0, U_F1IN, U_F1OUT)
            with sp.Fori(0, H // 2) as i:
                for j, col in enumerate((COL_Q, COL_K, COL_V)):
                    col_unit(U_QKV + j, w_in_mix[0], col + 256 * i, i, 3)
            with sp.Fori(0, G) as g:
                col_unit(U_SSD, w_in_mix[0], COL_X + 256 * g, g, 3)
                both = raw[:, (U_SSD + 1) % RAW, :].rearrange("p (k n) -> p k n", k=8)
                load(U_SSD + 1,
                     [(both[:, :, P * j:P * j + P],
                       w_in_mix[0][:, bass.ds(col + P * g, P)].rearrange("(k p) n -> p k n", p=P))
                      for j, col in enumerate((COL_B, COL_C))], g, 3)
                col_unit(U_SSD + 2, w_in_mix[0], COL_Z + 256 * g, g, 3)
            for u in range(4):
                col_unit(U_GA + u, w_in_mix[0], COL_GA + 256 * u)
            for u in range(4):
                row_unit(U_PA + u, proj_a[0], 256 * u)
            for u in range(8):
                row_unit(U_PB + u, proj_b[0], 256 * u)
            for u in range(4):
                col_unit(U_GB + u, w_in_mix[0], COL_GB + 256 * u)
            for u in range(4):
                row_unit(U_WO + u, w_out_mix[0], 256 * u)
            ffn(1, U_F2IN, U_F2OUT)
            for b in range(4):
                sp.wait_ge(out_copied, b + 1)
                sp.dma_start(out[0, :, 256 * b:256 * b + 256].rearrange("(s p) d -> p s d", p=P),
                             out_tok[:, b]).then_inc(stored, 16)
            sp.wait_ge(stored, 4 * 16)

        @block.gpsimd
        def _(pool):
            pool.memset(eps[:], EPS).then_inc(ones_set, 1)
            pool.memset(ones[:], 1.0).then_inc(ones_set, 1)
            pool.memset(ones_d[:], 1.0 / D).then_inc(ones_set, 1)
            pool.memset(ones_g[:], 1.0 / (HG * HP)).then_inc(ones_set, 1)

            def ada_src(chunk, k2):
                return w_ada[0][k2 * 256:(k2 + 1) * 256, bass.ds(chunk * D, D)].rearrange("(k p) n -> p k n", p=P)

            for j in range(8):
                if j >= 4:
                    pool.wait_ge(ada_used, j - 3)
                dst = ada_ring[:, j % 4, :] if j % 4 < 2 else scratch[:, (j % 4 - 2) * 2048:(j % 4 - 1) * 2048]
                pool.dma_start(dst.rearrange("p (k n) -> p k n", k=2), ada_src((SC1, SH1)[j // 4], j % 4)).then_inc(
                    ada_loaded[j % 4], 16)

            def ada_load(ch, j):
                pool.wait_ge(ada_used, 4 * ch + j - 1)
                pool.dma_start(ada_ring[:, j % 2, :].rearrange("p (k n) -> p k n", k=2),
                               ada_src(ch, j)).then_inc(ada_loaded[j % 2], 16)

            def add_part(f):
                for b in range(2):
                    pool.wait_ge(term_ready, KT * f + 2 * b + 2)
                    pool.tensor_tensor(hT[:, 2 * b:2 * b + 2, :], hT[:, 2 * b:2 * b + 2, :],
                                       work[:, 2 * b:2 * b + 2, :], ALU.add).then_inc(h_early, 1)
                if f == 2:
                    return
                m = 2 * f + 2
                for b in range(2):
                    pool.wait_ge(squared, 4 * m + b + 1)
                    pool.tensor_tensor(work[:, 2 * b, :], work[:, 2 * b, :], work[:, 2 * b + 1, :],
                                       ALU.add).then_inc(pair_early, 1)
                pool.wait_ge(pair_early, 2 * m)
                pool.tensor_tensor(work[:, 0, :], work[:, 0, :], work[:, 2, :], ALU.add).then_inc(quad_early, 1)

            pool.wait_ge(raw_loaded[1], 32)
            with pool.Fori(G1, SC2) as ch:
                for j in range(4):
                    ada_load(ch, j)
            ada_load(SC2, 0)
            ada_load(SC2, 1)
            add_part(0)
            ada_load(SC2, 2)
            ada_load(SC2, 3)
            pool.wait_ge(const_loaded, 16)
            pool.wait_ge(dt_done, 1)
            pool.tensor_copy(sel, ident[0:SH, 0:HG].unsqueeze(2).to_broadcast([SH, HG, P])).then_inc(sel_ready, 1)

            def y_gate(g):
                pool.wait_ge(y_skip, g + 1)
                pool.wait_ge(z_silu, g + 1)
                pool.tensor_tensor(yg, yg, ssm_z.rearrange("p (c t) -> p c t", c=2), ALU.mult).then_inc(y_gated, 1)

            def g_sum(g):
                pool.wait_ge(g_squared, g + 1)
                pool.tensor_tensor(gsq[:, 0, :], gsq[:, 0, :], gsq[:, 1, :], ALU.add).then_inc(g_summed, 1)

            def g_low(g):
                pool.wait_ge(g_hi, g + 1)
                pool.tensor_tensor(in_low[:, bass.ds(8 + 2 * g, 2), :], gsq,
                                   in_high[:, bass.ds(8 + 2 * g, 2), :].bitcast(F32), ALU.subtract).then_inc(g_lo, 1)

            def ssm(g):
                pool.wait_ge(ssd_cum, g)
                pool.tensor_copy(sel, ident[0:SH, bass.ds(HG * g, HG)].unsqueeze(2).to_broadcast([SH, HG, P])
                                 ).then_inc(sel_ready, 1)

            ssm(1)
            y_gate(0)
            g_sum(0)
            with pool.Fori(2, G) as g:
                ssm(g)
                g_low(g - 2)
                y_gate(g - 1)
                g_sum(g - 1)
            g_low(G - 2)
            y_gate(G - 1)
            g_sum(G - 1)
            g_low(G - 1)
            for j in range(4):
                ada_load(G2, j)
            add_part(1)
            add_part(2)

        @block.scalar
        def _(act):
            def split(n, i=0, step=0, halves=(0, 1)):
                if n >= UNITS:
                    return
                act.wait_ge(raw_loaded[n % RAW], 32 * (n // RAW + 1) + 32 * (step // RAW) * i)
                for g in halves:
                    if 2 * n + g >= GR:
                        act.wait_ge(used, split_count(n, g, i, step) - GR)
                    nc.scalar.activation(w_high[:, granule(n, g), :], raw[:, n % RAW, g * 1024:(g + 1) * 1024],
                                         ACT.Copy).then_inc(high_ready, 1)

            act.dma_start(rel_tab[:], rel_bias).then_inc(onehot_loaded, 16)
            act.dma_start(onehot, k_onehot).then_inc(onehot_loaded, 16)
            act.dma_start(causal, k_causal).then_inc(onehot_loaded, 16)

            act.wait_ge(c_turned, 1)
            nc.scalar.activation(cs[:], ps[:, 4, 0:KT], ACT.Silu).then_inc(cs_ready, 1)
            for b in range(4):
                act.wait_ge(x_turned, b + 1)
                nc.scalar.activation(hT[:, 2 * b:2 * b + 2, :], ps[:, b, :].rearrange("p (k t) -> p k t", k=2),
                                     ACT.Copy).then_inc(x_copied, 1)
            for b in range(4):
                act.wait_ge(x_copied, 4)
                act.wait_ge(x_turned, 4)
                nc.scalar.activation(work[:, 2 * b:2 * b + 2, :], hT[:, 2 * b:2 * b + 2, :],
                                     ACT.Square).then_inc(squared, 1)

            def root_table():
                nc.scalar.preload_act_table(ACT.Sqrt)

            def root(m, bank):
                act.wait_ge(mean_done, m + 1)
                nc.scalar.activation(rms[:], ps[:, bank, 0:T], ACT.Sqrt, bias=eps[:]).then_inc(root_ready, 1)

            def shift(f):
                if f == 0:
                    act.wait_ge(mod_ready, 2)
                for k in range(KT):
                    act.wait_ge(scaled, KT * f + k + 1)
                    nc.scalar.activation(u_high[:, k, :], work[:, k, :], ACT.Identity,
                                         bias=mod[:, 3 * f, k:k + 1]).then_inc(u_hi, 1)

            def after_part(f, bank, last=False):
                for b in range(4):
                    if b < 3:
                        act.wait_ge(part_done, 3 * f + b + 1)
                    else:
                        act.wait_ge(used, 2 * (U_QKV, U_F2IN, UNITS)[f])
                    nc.scalar.activation(work[:, 2 * b:2 * b + 2, :],
                                         ps[:, bank + b, :].rearrange("p (k t) -> p k t", k=2),
                                         ACT.Square).then_inc(squared, 1)
                split((U_QKV, U_F2IN, UNITS)[f] + 2, halves=(1,))
                root(2 * f + 1, 0)
                if last:
                    return
                for b in range(4):
                    act.wait_ge(h_early if b < 2 else h_late, 2 * f + b % 2 + 1)
                    nc.scalar.activation(work[:, 2 * b:2 * b + 2, :], hT[:, 2 * b:2 * b + 2, :],
                                         ACT.Square).then_inc(squared, 1)
                root(2 * f + 2, 1)

            def ffn(f, u_in, u_out):
                def pair(p, i=0):
                    n = u_in + 2 * p
                    split(n + 3, i, 6)
                    split(n + 4, i, 6)
                    act.wait_ge(used, 2 * n + 4 + 12 * i)
                    if f == 0 and p == 0:
                        act.wait_ge(par_turned, 3)
                    nc.scalar.activation(silu_a[:, p % 3, :], ps[:, 2 * (p % 3), :], ACT.Silu).then_inc(silu_done, 1)
                    act.wait_ge(s_done, PAIRS * f + p + 1 + 3 * i)
                    nc.scalar.activation(in_high[:, bass.ds(2 * p + 6 * i, 2), :],
                                         silu_a[:, p % 3, :].rearrange("p (k t) -> p k t", k=2),
                                         ACT.Copy).then_inc(s_hi, 1)

                pair(0)
                pair(1)
                with act.Fori(0, (PAIRS - 2) // 3) as i:
                    for p in range(2, 5):
                        pair(p, i)
                root_table()
                if f == 0:
                    with act.Fori(0, PAIRS // 3) as i:
                        for u in range(3):
                            split(u_out + u + 3, i, 3)
                    for u in range(PAIRS // 3 * 3, PAIRS - 1):
                        split(u_out + u + 3)
                    split(u_out + PAIRS + 2, halves=(0,))
                else:
                    with act.Fori(0, (PAIRS - 3) // 3) as i:
                        for u in range(3):
                            split(u_out + u + 3, i, 3)
                    for u in range((PAIRS - 3) // 3 * 3, PAIRS):
                        split(u_out + u + 3)

            def dt_chain():
                act.wait_ge(dt_in, 1)
                nc.scalar.activation(dts[:, 1], dts[:, 0], ACT.Abs).then_inc(dt_act, 1)
                act.wait_ge(dt_act, 1)
                nc.scalar.activation(dts[:, 2], dts[:, 1], ACT.Exp, scale=-1.0).then_inc(dt_act, 1)
                nc.scalar.activation(aexp[:], aexp[:], ACT.Exp).then_inc(dt_act, 1)
                act.wait_ge(dt_act, 3)
                nc.scalar.activation(dts[:, 3], dts[:, 2], ACT.Ln, bias=1.0).then_inc(dt_act, 1)

            def turn_copy(i):
                act.wait_ge(probs_turned, i + 1)
                nc.scalar.activation(probsT, ps[:, 5:7, 0:384], ACT.Copy).then_inc(probsT_ready, 1)

            def o_split(i):
                act.wait_ge(pv_done, i + 1)
                nc.scalar.activation(in_high[:, bass.ds(2 * i, 2), :],
                                     ps[:, 7, :].rearrange("p (h q) -> p h q", h=2), ACT.Copy).then_inc(o_hi, 1)

            def attention(i, first):
                n, r = U_QKV, (0 if first else i)
                split(n + 3, r, 3)
                act.wait_ge(used, 2 * n + 2 + 6 * r)
                nc.scalar.activation(qT, ps[:, 0, :].rearrange("p (h q) -> p h q", h=2), ACT.Copy,
                                     scale=float(P) ** -0.5).then_inc(q_copied, 1)
                if first:
                    dt_chain()
                split(n + 4, r, 3)
                if not first:
                    turn_copy(i - 1)
                split(n + 5, r, 3)
                act.wait_ge(used, 2 * n + 6 + 6 * r)
                nc.scalar.activation(vT, ps[:, 2, :].rearrange("p (h q) -> p h q", h=2),
                                     ACT.Copy).then_inc(v_copied, 1)
                if first:
                    act.wait_ge(cum_turned, 1)
                    nc.scalar.activation(cum_high[:], ps[0:SH, 6, 0:T], ACT.Copy).then_inc(cum_hi, 1)
                else:
                    o_split(i - 1)
                act.wait_ge(max_ready, i + 1)
                for j in range(4):
                    part = probs[:, j % 2, 0:256] if j < 2 else probs[:, j % 2, 256:384]
                    ins = nc.scalar.activation(part, part, ACT.Exp, bias=nmax[:, j:j + 1],
                                               accum_out=rsum[:, j:j + 1])
                ins.then_inc(exp_done, 1)

            def decays(g):
                act.wait_ge(ssd_cum, g + 1)
                for j in range(HG):
                    run = ps[:, 5 + j // 2, 256 * (j % 2):256 * (j % 2) + 256]
                    nc.scalar.activation(decay[:, j, 0:256], run, ACT.Relu, scale=-1.0,
                                         bias=cum[:, 0, bass.ds(HG * g + j, 1)])
                    ins = nc.scalar.activation(decay[:, j, 256:384], run[:, 128:256], ACT.Relu, scale=-1.0,
                                               bias=cum[:, 1, bass.ds(HG * g + j, 1)])
                ins.then_inc(seg_done, 1)
                act.wait_ge(seg_done, g + 1)
                nc.scalar.activation(decay, decay, ACT.Exp, scale=-1.0).then_inc(decay_ready, 1)

            def tap(bank, j, tile):
                nc.scalar.activation(conv[:, j, :], ps[:, bank, 256 * (j % 2):256 * (j % 2) + 256], ACT.Identity,
                                     scale=par2[:, TAPS - 1, tile], bias=par3[:, tile]).then_inc(tap_done, 1)

            def z_gate(g):
                act.wait_ge(used, 2 * U_SSD + 6 + 6 * g)
                nc.scalar.activation(ssm_z, ps[:, 2, :], ACT.Silu).then_inc(z_silu, 1)

            def g_square(g, busy=True):
                act.wait_ge(y_gated, g + 1)
                if busy:
                    act.wait_ge(g_lo, g)
                nc.scalar.activation(gsq, yg, ACT.Square).then_inc(g_squared, 1)

            def g_root_guess(g):
                nc.scalar.preload_act_table_set("natural_log_exp_and_others")
                act.wait_ge(g_mean, g + 1)
                nc.scalar.activation(rms_g, ps[:, 7, 0:T], ACT.Ln, bias=eps[:]).then_inc(g_log, 1)
                act.wait_ge(g_log, g + 1)
                nc.scalar.activation(rms_g, rms_g, ACT.Exp, scale=-0.5).then_inc(g_root, 1)

            def g_split(g):
                act.wait_ge(g_normed, g + 1)
                nc.scalar.activation(in_high[:, bass.ds(8 + 2 * g, 2), :], gsq, ACT.Copy).then_inc(g_hi, 1)

            def ssm(g):
                count = g if isinstance(g, int) else 2
                n = U_SSD
                if count >= 2:
                    g_root_guess(g - 2)
                if count >= 1:
                    decays(g - 1)
                if count >= 2:
                    g_split(g - 2)
                split(n + 3, g, 3)
                if count == 0:
                    turn_copy(H // 2 - 1)
                act.wait_ge(used, 2 * n + 2 + 6 * g)
                if count == 0:
                    act.wait_ge(probs_ready, H // 2)
                else:
                    act.wait_ge(skip_ready, g)
                tap(0, 0, bass.ds(2 * g, 1))
                tap(0, 1, bass.ds(2 * g + 1, 1))
                if count >= 1:
                    z_gate(g - 1)
                if count == 0:
                    o_split(H // 2 - 1)
                act.wait_ge(used, 2 * n + 4 + 6 * g)
                tap(1, 2, bass.ds(16 + g, 1))
                tap(1, 3, bass.ds(24 + g, 1))
                act.wait_ge(conv_done, 2 * g + 1)
                nc.scalar.activation(conv[:, 0:2, :], conv[:, 0:2, :], ACT.Silu).then_inc(conv_silu, 1)
                split(n + 4, g, 3)
                if count >= 1:
                    g_square(g - 1, count >= 2)
                act.wait_ge(conv_done, 2 * g + 2)
                nc.scalar.activation(conv[:, 2:4, :], conv[:, 2:4, :], ACT.Silu).then_inc(conv_silu, 1)
                split(n + 5, g, 3)

            root_table()
            root(0, 6)
            for j in range(2):
                act.wait_ge(ada_loaded[j], 32)
                nc.scalar.activation(ada_parts[:, j, :], ada_ring[:, j, D:2 * D], ACT.Identity,
                                     scale=cs[:, 2 * j + 1:2 * j + 2]).then_inc(ada_scaled, 1)
            act.wait_ge(bias_copied, 1)
            act.dma_start(bias_rows, causal).then_inc(bias_stored, 16)
            split(0)
            shift(0)
            split(1)
            split(2)
            act.wait_ge(small_loaded, 10 * 16)
            nc.scalar.activation(dtw_high, dtw[:], ACT.Copy).then_inc(dtw_hi, 1)
            act.wait_ge(bias_stored, 16)
            act.wait_ge(ada_used, 8)
            act.dma_start(hankel, bass.AP(bias_rows.tensor, 0, [[1, P], [384, H], [1, T]])).then_inc(hankel_loaded, 16)

            ffn(0, U_F1IN, U_F1OUT)
            after_part(0, 4)
            shift(1)
            act.wait_ge(toep_turned, 1)
            for b in range(4):
                nc.scalar.activation(toep[:, 2 * b:2 * b + 2, :], ps[:, 4 + b, :].rearrange("p (h k) -> p h k", h=2),
                                     ACT.Copy).then_inc(toep_ready, 1)
            attention(0, True)
            with act.Fori(1, H // 2) as i:
                attention(i, False)
            ssm(0)
            ssm(1)
            with act.Fori(2, G) as g:
                ssm(g)
            g_root_guess(G - 2)
            decays(G - 1)
            g_split(G - 2)
            for u in range(4):
                split(U_GA + u + 3)
                if u == 0:
                    z_gate(G - 1)
                if u == 2:
                    g_square(G - 1)
                act.wait_ge(used, 2 * (U_GA + u) + 2)
                nc.scalar.activation(work[:, 2 * u:2 * u + 2, :],
                                     ps[:, GA_BANK[u], :].rearrange("p (k t) -> p k t", k=2),
                                     ACT.Sigmoid).then_inc(gate_a_done, 1)
            g_root_guess(G - 1)
            g_split(G - 1)
            for n in range(U_PA, U_GB):
                split(n + 3)
            for u in range(4):
                split(U_GB + u + 3)
                act.wait_ge(used, 2 * (U_GB + u) + 2)
                if u >= 2:
                    act.wait_ge(gate_b_used, u - 1)
                nc.scalar.activation(gate_b[:, u % 2, :], ps[:, u % 2, :], ACT.Sigmoid).then_inc(gate_b_done, 1)
                act.wait_ge(mixed_b, u + 1)
                nc.scalar.activation(in_high[:, 2 * u:2 * u + 2, :], work[:, 2 * u:2 * u + 2, :],
                                     ACT.Copy).then_inc(m_hi, 1)
            for n in range(U_WO, U_F2IN - 1):
                split(n + 3)
            root_table()
            split(U_F2IN + 2, halves=(0,))
            after_part(1, 2)
            shift(2)
            ffn(1, U_F2IN, U_F2OUT)
            after_part(2, 4, last=True)
            for b in range(4):
                act.wait_ge(out_turned, b + 1)
                nc.scalar.activation(out_tok[:, b], ps[:, b, :].rearrange("p (s d) -> p s d", s=2),
                                     ACT.Copy).then_inc(out_copied, 1)

        @block.vector
        def _(dve):
            done = [0]

            def after(ins):
                done[0] += 1
                ins.then_inc(own, 1)
                dve.wait_ge(own, done[0])

            def split(n, i=0, step=0, halves=(0, 1)):
                if n >= UNITS:
                    return
                for g in halves:
                    dve.wait_ge(high_ready, split_count(n, g, i, step))
                    dve.tensor_tensor(w_low[:, granule(n, g), :], raw[:, n % RAW, g * 1024:(g + 1) * 1024],
                                      w_high[:, granule(n, g), :].bitcast(F32), ALU.subtract).then_inc(low_ready, 1)

            def ada_unit(ch, j, i=0):
                acc = {1: ada_acc1, SH2: ada_acc_sh2, G2: ada_acc_g2}.get(ch, ada_acc[:])
                if ch < 2:
                    slot, count = j, 16 * (ch + 1)
                else:
                    slot = j % 2
                    count = 16 * (2 + 2 * (ch - 2) + j // 2 + 1) + 32 * i
                src = ada_ring[:, slot, :] if slot < 2 else scratch[:, (slot - 2) * 2048:(slot - 1) * 2048]
                dve.wait_ge(ada_loaded[slot], count)
                if j == 0 and ch >= 2 and ch not in (SH2, G2):
                    dve.wait_ge(ada_summed, ch + i)
                step = 8 * ch + 2 * j + 8 * i
                if ch == 1:
                    step -= min(j, 2)
                elif ch > 1:
                    step -= 2
                for k in range(1 if ch == 1 and j < 2 else 2):
                    part, col = src[:, k * D:(k + 1) * D], cs[:, 2 * j + k:2 * j + k + 1]
                    if j == 0 and k == 0:
                        ins = dve.tensor_scalar(acc, part, col, None, ALU.mult)
                    else:
                        dve.wait_ge(ada_step, step)
                        ins = dve.scalar_tensor_tensor(out=acc, in0=part, scalar=col, in1=acc,
                                                       op0=ALU.mult, op1=ALU.add)
                    ins.then_inc(ada_step, 1)
                    step = step + 1
                dve.wait_ge(ada_step, step)
                if ch == 1 and j < 2:
                    dve.wait_ge(ada_scaled, j + 1)
                dve.sem_inc(ada_used, 1)
                if j == 3:
                    dve.sem_inc(ada_ready, 1)

            def ada_take(ch, bank, i=0, nth=None):
                dve.wait_ge(ada_summed, (ch if nth is None else nth) + 1 + i)
                dve.tensor_tensor(mod[:, bass.ds(ch + i, 1), :].rearrange("p a k -> p (a k)"), ps[:, bank, 0:KT],
                                  par1[:, bass.ds(KT + KT * ch + KT * i, KT)], ALU.add).then_inc(mod_ready, 1)

            def gain(m):
                return par1[:, 80 + 8 * m:88 + 8 * m]

            def make_scale_in(f):
                dve.wait_ge(mod_ready, 3 * f + 2 if f else 1)
                after(dve.scalar_tensor_tensor(out=scale_in[:, f, :], in0=mod[:, 3 * f + 1, :], scalar=1.0,
                                               in1=gain(2 * f), op0=ALU.add, op1=ALU.mult))

            def make_scale_out(f):
                dve.wait_ge(mod_ready, 3 * f + 3)
                after(dve.scalar_tensor_tensor(out=scale_out[:, f, :], in0=mod[:, 3 * f + 2, :],
                                               scalar=1.0 if f == 1 else 0.5, in1=gain(2 * f + 1),
                                               op0=ALU.mult, op1=ALU.mult))

            def add_squares(m):
                for q, pair, quad in ((0, pair_early, quad_early), (1, pair_late, quad_late)):
                    if q == 0 and m % 2 == 0:
                        continue
                    for b in (2 * q, 2 * q + 1):
                        dve.wait_ge(squared, 4 * m + b + 1)
                        dve.tensor_tensor(work[:, 2 * b, :], work[:, 2 * b, :], work[:, 2 * b + 1, :],
                                          ALU.add).then_inc(pair, 1)
                    dve.wait_ge(pair, 2 * m)
                    dve.tensor_tensor(work[:, 4 * q, :], work[:, 4 * q, :], work[:, 4 * q + 2, :],
                                      ALU.add).then_inc(quad, 1)

            def make_rms(m):
                dve.wait_ge(root_ready, m + 1)
                dve.reciprocal(rms[:], rms[:]).then_inc(rms_ready, 1)
                dve.wait_ge(rms_ready, m + 1)

            def in_norm(f):
                if f:
                    add_squares(2 * f)
                    make_rms(2 * f)

                def low(k):
                    dve.wait_ge(u_hi, KT * f + k + 1)
                    dve.scalar_tensor_tensor(out=u_low[:, k, :], in0=work[:, k, :], scalar=mod[:, 3 * f, k:k + 1],
                                             in1=u_high[:, k, :].bitcast(F32), op0=ALU.add,
                                             op1=ALU.subtract).then_inc(u_lo, 1)

                def scale(k):
                    dve.scalar_tensor_tensor(out=work[:, k, :], in0=hT[:, k, :], scalar=scale_in[:, f, k:k + 1],
                                             in1=rms[:], op0=ALU.mult, op1=ALU.mult).then_inc(scaled, 1)

                if f:
                    for k in range(KT):
                        scale(k)
                        if k >= 2:
                            low(k - 2)
                    low(KT - 2)
                    low(KT - 1)
                    return
                for k in range(KT - 2):
                    scale(k)
                    if k == 3:
                        split(0, halves=(0,))
                ada_take(SH1, 7, nth=1)
                for k in range(KT):
                    low(k)
                    if k in (1, 2):
                        scale(k + KT - 3)
                    if k == 3:
                        split(0, halves=(1,))

            def scale_part(f, bank):
                if f == 2:
                    add_squares(5)
                make_rms(2 * f + 1)
                for k in range(KT):
                    dve.scalar_tensor_tensor(out=work[:, k, :],
                                             in0=ps[:, bank + k // 2, T * (k % 2):T * (k % 2) + T],
                                             scalar=scale_out[:, f, k:k + 1], in1=rms[:], op0=ALU.mult,
                                             op1=ALU.mult).then_inc(term_ready, 1)
                    if k in (5, 7):
                        dve.wait_ge(term_ready, KT * f + k + 1)
                        dve.tensor_tensor(hT[:, k - 1:k + 1, :], hT[:, k - 1:k + 1, :], work[:, k - 1:k + 1, :],
                                          ALU.add).then_inc(h_late, 1)

            def ffn(f, u_in, u_out):
                def gate(p, i=0):
                    dve.wait_ge(silu_done, PAIRS * f + p + 1 + 3 * i)
                    dve.tensor_tensor(silu_a[:, p % 3, :], silu_a[:, p % 3, :], ps[:, 2 * (p % 3) + 1, :],
                                      ALU.mult).then_inc(s_done, 1)

                def low(p, i=0):
                    dve.wait_ge(s_hi, PAIRS * f + p + 1 + 3 * i)
                    dve.tensor_tensor(in_low[:, bass.ds(2 * p + 6 * i, 2), :],
                                      silu_a[:, p % 3, :].rearrange("p (k t) -> p k t", k=2),
                                      in_high[:, bass.ds(2 * p + 6 * i, 2), :].bitcast(F32),
                                      ALU.subtract).then_inc(s_lo, 1)

                for p in range(2):
                    split(u_in + 2 * p + 3)
                    split(u_in + 2 * p + 4)
                    gate(p)
                    if f == 0:
                        ada_unit(G1, 2 * p)
                        ada_unit(G1, 2 * p + 1)
                    low(p)
                with dve.Fori(0, (PAIRS - 2) // 3) as i:
                    for p in range(2, 5):
                        n = u_in + 2 * p
                        split(n + 3, i, 6)
                        split(n + 4, i, 6)
                        gate(p, i)
                        if f == 0 and p == 3:
                            ada_take(G1, 7, i)
                            ada_unit(SHM, 0, i)
                            ada_unit(SHM, 1, i)
                        if f == 0 and p == 4:
                            ada_unit(SHM, 2, i)
                            ada_unit(SHM, 3, i)
                        low(p, i)
                if f == 1:
                    end = (PAIRS - 3) // 3 * 3
                    with dve.Fori(0, end // 3) as i:
                        for u in range(3):
                            split(u_out + u + 3, i, 3)
                    for u in range(end, PAIRS):
                        split(u_out + u + 3)
                    return
                ada_after = {2: [(SH2, 0)], 3: [(SH2, 1)], 4: [(SH2, 2)], 5: [(SH2, 3)]}
                for u in range(PAIRS - 1):
                    split(u_out + u + 3)
                    if u == 2:
                        make_scale_out(0)
                        make_scale_in(1)
                    for ch, j in ada_after.get(u, ()):
                        ada_unit(ch, j)
                add_squares(1)

            def turn_copy(i):
                dve.wait_ge(probs_turned, i + 1)
                dve.tensor_copy(v_tok, ps[:, 7, :].rearrange("p (h s d) -> p h s d", h=2, s=2)).then_inc(v_ready, 1)

            def o_split(i):
                dve.wait_ge(o_hi, i + 1)
                dve.tensor_tensor(in_low[:, bass.ds(2 * i, 2), :], ps[:, 7, :].rearrange("p (h q) -> p h q", h=2),
                                  in_high[:, bass.ds(2 * i, 2), :].bitcast(F32), ALU.subtract).then_inc(o_lo, 1)

            def dt_chain():
                dve.wait_ge(dt_done, 1)
                dve.tensor_tensor(dts[:, 0], ps[:, 5, 0:2 * SH].rearrange("p (s h) -> p s h", s=2),
                                  dtb[:].unsqueeze(1).to_broadcast([P, 2, SH]), ALU.add).then_inc(dt_in, 1)
                dve.wait_ge(dt_in, 1)
                dve.wait_ge(dt_act, 4)
                after(dve.tensor_scalar(dts[:, 1], dts[:, 0], 0.0, None, ALU.max))
                after(dve.tensor_tensor(dt[:], dts[:, 1], dts[:, 3], ALU.add))
                dve.scalar_tensor_tensor(out=dts[:, 2], in0=dt[:], scalar=-1.0,
                                         in1=aexp[:].unsqueeze(1).to_broadcast([P, 2, SH]), op0=ALU.mult,
                                         op1=ALU.mult).then_inc(dt_ready, 1)

            def attention(i, first):
                n, r = U_QKV, (0 if first else i)
                split(n + 3, r, 3)
                if first:
                    dt_chain()
                    ada_unit(SC2, 0)
                split(n + 4, r, 3)
                dve.wait_ge(used, 2 * n + 4 + 6 * r)
                dve.tensor_copy(kTt, ps[:, 1, :].rearrange("p (h q) -> p h q", h=2)).then_inc(k_copied, 1)
                if not first:
                    turn_copy(i - 1)
                if first:
                    ada_unit(SC2, 1)
                split(n + 5, r, 3)
                if first:
                    dve.wait_ge(cum_done, 1)
                    dve.tensor_copy(cum[:], ps[:, 5, 2 * SH:4 * SH].rearrange("p (s h) -> p s h", s=2)
                                    ).then_inc(cum_copied, 1)
                    dve.wait_ge(toep_ready, 4)
                dve.wait_ge(scores_done, i + 1)
                dve.tensor_tensor(probs[:, :, 0:256], ps[:, 3:5, 0:256], toep[:, bass.ds(2 * i, 2), :],
                                  ALU.add).then_inc(softmax_step, 1)
                dve.tensor_tensor(probs[:, :, 256:384], ps[:, 3:5, 256:384], toep[:, bass.ds(2 * i, 2), 128:256],
                                  ALU.add).then_inc(softmax_step, 1)
                dve.wait_ge(softmax_step, 7 * i + 2)
                dve.tensor_reduce(rsum[:, 0:2], probs[:, :, 0:256], AX_X, ALU.max).then_inc(softmax_step, 1)
                dve.tensor_reduce(rsum[:, 2:4], probs[:, :, 256:384], AX_X, ALU.max).then_inc(softmax_step, 1)
                dve.wait_ge(softmax_step, 7 * i + 4)
                dve.tensor_scalar(nmax[:], rsum[:], -1.0, None, ALU.mult).then_inc(max_ready, 1)
                if first:
                    dve.wait_ge(cum_hi, 1)
                    dve.tensor_tensor(cum_low[:], ps[0:SH, 6, 0:T], cum_high[:].bitcast(F32),
                                      ALU.subtract).then_inc(cum_lo, 1)
                else:
                    o_split(i - 1)
                dve.wait_ge(exp_done, i + 1)
                dve.reciprocal(rsum[:], rsum[:]).then_inc(softmax_step, 1)
                dve.wait_ge(softmax_step, 7 * i + 5)
                dve.tensor_tensor(probs[:, :, 0:256], probs[:, :, 0:256],
                                  rsum[:, 0:2].unsqueeze(2).to_broadcast([P, 2, 256]),
                                  ALU.mult).then_inc(softmax_step, 1)
                dve.tensor_tensor(probs[:, :, 256:384], probs[:, :, 256:384],
                                  rsum[:, 2:4].unsqueeze(2).to_broadcast([P, 2, 128]),
                                  ALU.mult).then_inc(softmax_step, 1)
                dve.wait_ge(softmax_step, 7 * i + 7)
                dve.sem_inc(probs_ready, 1)
                if first:
                    ada_unit(SC2, 2)
                    ada_unit(SC2, 3)

            def weights(g):
                dve.wait_ge(decay_ready, g + 1)
                dve.wait_ge(cbm_ready, g + 1)
                dve.tensor_tensor(decay, decay, cbm.unsqueeze(1).to_broadcast([P, HG, 384]),
                                  ALU.mult).then_inc(w_ready, 1)

            def taps(bank, j0, tiles, half, g):
                for t in range(1, TAPS):
                    for j in range(2):
                        if t == 1:
                            dve.wait_ge(tap_done, 4 * g + j0 + 2)
                        else:
                            dve.wait_ge(taps_step, 12 * g + 6 * half + 2 * (t - 2) + j + 1)
                        dve.scalar_tensor_tensor(out=conv[:, j0 + j, t:T], in0=ps[:, bank, T * j:T * j + T - t],
                                                 scalar=par2[:, TAPS - 1 - t, tiles[j]],
                                                 in1=conv[:, j0 + j, t:T], op0=ALU.mult,
                                                 op1=ALU.add).then_inc(taps_step, 1)
                dve.wait_ge(taps_step, 12 * g + 6 * half + 6)
                dve.sem_inc(conv_done, 1)

            def x_skip(g, busy=True):
                if busy:
                    dve.wait_ge(g_normed, g)
                dve.wait_ge(conv_silu, 2 * g + 1)
                for q in range(2):
                    ins = dve.tensor_scalar(yg[:, q, :], conv[:, q, :], dskip[:, bass.ds(2 * g + q, 1)], None,
                                            ALU.mult)
                ins.then_inc(skip_ready, 1)

            def y_take(g):
                dve.wait_ge(y_done, g + 1)
                dve.wait_ge(skip_ready, g + 1)
                dve.tensor_tensor(yg, yg, ps[:, 7, :].rearrange("p (c t) -> p c t", c=2), ALU.add).then_inc(y_skip, 1)

            def g_norm(g):
                dve.wait_ge(g_root, g + 1)
                dve.scalar_tensor_tensor(out=newton, in0=ps[:, 7, 0:T], scalar=EPS, in1=rms_g, op0=ALU.add,
                                         op1=ALU.mult).then_inc(g_newton, 1)
                dve.wait_ge(g_newton, 2 * g + 1)
                dve.scalar_tensor_tensor(out=newton, in0=newton, scalar=-0.5, in1=rms_g, op0=ALU.mult,
                                         op1=ALU.mult).then_inc(g_newton, 1)
                dve.wait_ge(g_newton, 2 * g + 2)
                dve.scalar_tensor_tensor(out=rms_g, in0=newton, scalar=1.5, in1=rms_g, op0=ALU.add,
                                         op1=ALU.mult).then_inc(g_rms, 1)
                dve.wait_ge(g_rms, g + 1)
                for q in range(2):
                    ins = dve.scalar_tensor_tensor(out=gsq[:, q, :], in0=yg[:, q, :],
                                                   scalar=par3[:, bass.ds(32 + 2 * g + q, 1)], in1=rms_g,
                                                   op0=ALU.mult, op1=ALU.mult)
                ins.then_inc(g_normed, 1)

            def ssm(g):
                count = g if isinstance(g, int) else 2
                n = U_SSD
                if count >= 2:
                    g_norm(g - 2)
                if count >= 1:
                    x_skip(g - 1, count >= 2)
                    weights(g - 1)
                split(n + 3, g, 3)
                if count == 0:
                    turn_copy(H // 2 - 1)
                taps(0, 0, (bass.ds(2 * g, 1), bass.ds(2 * g + 1, 1)), 0, g)
                if count == 0:
                    o_split(H // 2 - 1)
                else:
                    y_take(g - 1)
                taps(1, 2, (bass.ds(16 + g, 1), bass.ds(24 + g, 1)), 1, g)
                split(n + 4, g, 3)
                split(n + 5, g, 3)
                dve.wait_ge(ssd_in, g + 1)
                dve.tensor_tensor(xdt, ps[:, 4, :].rearrange("p (s h d) -> p s h d", s=2, h=HG),
                                  dt[:, :, bass.ds(HG * g, HG)].unsqueeze(3).to_broadcast([P, 2, HG, HP]),
                                  ALU.mult).then_inc(xdt_ready, 1)
                dve.tensor_tensor(cbm, ps[:, 3, 0:384], mask[:], ALU.mult).then_inc(cbm_ready, 1)

            dve.wait_ge(cs_ready, 1)
            for j in range(4):
                ada_unit(0, j)
            dve.wait_ge(par_turned, 1)
            dve.tensor_copy(par1[:], ps[:, 4, 0:P]).then_inc(par_copied, 1)
            ada_unit(1, 0)
            make_rms(0)
            ada_unit(1, 1)
            dve.wait_ge(bias_made, 1)
            dve.tensor_tensor(causal, causal, ps[0:H, 5, 0:384], ALU.add).then_inc(bias_copied, 1)
            dve.wait_ge(par_copied, 1)
            ada_take(SC1, 7, nth=0)
            make_scale_in(0)
            ada_unit(1, 2)
            ada_unit(1, 3)
            in_norm(0)
            split(1)
            dve.wait_ge(par_turned, 3)
            dve.tensor_copy(par2[:].rearrange("p t r -> p (t r)"), ps[:, 4, P:2 * P]).then_inc(par_copied, 1)
            dve.tensor_copy(par3[:], ps[:, 4, 2 * P:2 * P + 48]).then_inc(par_copied, 1)
            split(2)
            dve.wait_ge(dtw_hi, 1)
            dve.tensor_tensor(dtw_low, dtw[:], dtw_high.bitcast(F32), ALU.subtract).then_inc(dtw_lo, 1)
            ffn(0, U_F1IN, U_F1OUT)
            scale_part(0, 4)
            in_norm(1)
            split(U_QKV + 2)
            ada_take(GM, 2)
            ada_take(SH2, 3)
            make_scale_out(1)
            attention(0, True)
            with dve.Fori(1, H // 2) as i:
                attention(i, False)
            ssm(0)
            ssm(1)
            with dve.Fori(2, G) as g:
                ssm(g)
            g_norm(G - 2)
            x_skip(G - 1)
            weights(G - 1)
            for u in range(4):
                split(U_GA + u + 3)
                if u == 1:
                    y_take(G - 1)
            g_norm(G - 1)
            for u in range(4):
                split(U_PA + u + 3)
            for b in range(4):
                dve.wait_ge(used, 2 * U_PB)
                dve.tensor_tensor(work[:, 2 * b:2 * b + 2, :], work[:, 2 * b:2 * b + 2, :],
                                  ps[:, b, :].rearrange("p (k t) -> p k t", k=2), ALU.mult).then_inc(mixed_a, 1)
            for u in range(8):
                split(U_PB + u + 3)
                if 1 <= u < 5:
                    ada_unit(G2, u - 1)

            def m_split(u):
                dve.wait_ge(m_hi, u + 1)
                dve.tensor_tensor(in_low[:, 2 * u:2 * u + 2, :], work[:, 2 * u:2 * u + 2, :],
                                  in_high[:, 2 * u:2 * u + 2, :].bitcast(F32), ALU.subtract).then_inc(m_lo, 1)

            for u in range(4):
                split(U_GB + u + 3)
                dve.wait_ge(gate_b_done, u + 1)
                dve.tensor_tensor(gate_b[:, u % 2, :], gate_b[:, u % 2, :], ps[:, 4 + u, :],
                                  ALU.mult).then_inc(gate_b_used, 1)
                dve.wait_ge(gate_b_used, u + 1)
                dve.tensor_tensor(work[:, 2 * u:2 * u + 2, :], work[:, 2 * u:2 * u + 2, :],
                                  gate_b[:, u % 2, :].rearrange("p (k t) -> p k t", k=2),
                                  ALU.add).then_inc(mixed_b, 1)
                dve.wait_ge(mixed_b, u + 1)
                m_split(u)
            for n in range(U_WO, U_F2IN - 1):
                split(n + 3)
            add_squares(3)
            scale_part(1, 2)
            ada_take(SC2, 6)
            make_scale_in(2)
            in_norm(2)
            split(U_F2IN + 2)
            ada_take(G2, 7)
            make_scale_out(2)
            ffn(1, U_F2IN, U_F2OUT)
            scale_part(2, 4)

        @block.tensor
        def _(pe):
            def three(out, k_high, k_low, x_high, x_low, start, stop):
                pe.matmul(out, k_high, x_high, start=start, stop=False, skip_group_check=True)
                pe.matmul(out, k_high, x_low, start=False, stop=False, skip_group_check=True)
                return pe.matmul(out, k_low, x_high, start=False, stop=stop, skip_group_check=True)

            def col_unit(n, bank, i=0, step=0, fresh=None):
                for g in range(2):
                    pe.wait_ge(low_ready, split_count(n, g, i, step))
                    wh = w_high[:, granule(n, g), :].rearrange("p (k n) -> p k n", k=4)
                    wl = w_low[:, granule(n, g), :].rearrange("p (k n) -> p k n", k=4)
                    for k in range(4):
                        kt = 4 * g + k
                        if fresh is not None:
                            pe.wait_ge(u_lo, fresh + kt + 1)
                        for c2 in range(2):
                            ins = three(ps[:, bank, T * c2:T * c2 + T], wh[:, k, P * c2:P * c2 + P],
                                        wl[:, k, P * c2:P * c2 + P], u_high[:, kt, :], u_low[:, kt, :],
                                        kt == 0 and c2 == 0, kt == KT - 1)
                    ins.then_inc(used, 1)

            def row_unit(n, bank, kt, first, last, i=0, step=0, completes=False):
                for g in range(2):
                    pe.wait_ge(low_ready, split_count(n, g, i, step))
                    for m in range(8):
                        at = slice(P * m, P * m + P)
                        ins = three(ps[:, bank + m // 2, T * (m % 2):T * (m % 2) + T],
                                    w_high[:, granule(n, g), at], w_low[:, granule(n, g), at],
                                    in_high[:, bass.ds(kt + g, 1), :].rearrange("p a t -> p (a t)"),
                                    in_low[:, bass.ds(kt + g, 1), :].rearrange("p a t -> p (a t)"),
                                    first and g == 0 and m % 2 == 0, last and g == 1)
                        if completes and g == 1 and m in (1, 3, 5):
                            ins.then_inc(part_done, 1)
                    ins.then_inc(used, 1)

            def mean(m, bank):
                for q in range(2):
                    pe.wait_ge((quad_early, quad_late)[q], m)
                    ins = pe.matmul(ps[:, bank, 0:T], ones_d[:], work[:, 4 * q, :], start=(q == 0), stop=(q == 1),
                                    skip_group_check=True)
                ins.then_inc(mean_done, 1)

            def ada_sum(ch, bank, i=0):
                acc = {1: ada_acc1, SH2: ada_acc_sh2, G2: ada_acc_g2}.get(ch, ada_acc[:])
                if ch == 1:
                    for j in range(2):
                        pe.wait_ge(ada_scaled, j + 1)
                        for k in range(KT):
                            ins = pe.matmul(ps[:, bank, k:k + 1], ada_parts[:, j, P * k:P * k + P], ones[:, 0:1],
                                            start=(j == 0 and k == 0), stop=False, skip_group_check=True)
                    ins.then_inc(parts_summed, 1)
                pe.wait_ge(ada_ready, ch + 1 + i)
                for k in range(KT):
                    ins = pe.matmul(ps[:, bank, k:k + 1], acc[:, P * k:P * k + P], ones[:, 0:1],
                                    start=(ch != 1), stop=True, skip_group_check=True)
                ins.then_inc(ada_summed, 1)

            def ffn(f, u_in, u_out):
                def pair(p, i=0):
                    if p >= 2:
                        pe.wait_ge(s_done, PAIRS * f + p - 1 + 3 * i)
                    col_unit(u_in + 2 * p, 2 * (p % 3), i, 6, KT * (0, 2)[f] if p == 0 else None)
                    if f == 0 and p == 0:
                        pe.wait_ge(small_loaded, 10 * 16)
                        pe.transpose(ps[:, 4, P:2 * P], par[:, 1, :], ident[:]).then_inc(par_turned, 1)
                        pe.transpose(ps[:, 4, 2 * P:2 * P + 48], par[0:48, 2, :],
                                     ident[0:48, 0:48]).then_inc(par_turned, 1)
                    if f == 0 and p == 3:
                        ada_sum(G1, 7, i)
                    col_unit(u_in + 2 * p + 1, 2 * (p % 3) + 1, i, 6)

                def out_unit(u, i=0):
                    pe.wait_ge(s_lo, PAIRS * f + u + 1 + 3 * i)
                    row_unit(u_out + u, 4, 2 * u + 6 * i, u == 0, u == PAIRS - 1, i, 3,
                             completes=(u == PAIRS - 1))

                pair(0)
                pair(1)
                if f == 0:
                    pe.wait_ge(par_copied, 3)
                    pe.wait_ge(bias_copied, 1)
                with pe.Fori(0, (PAIRS - 2) // 3) as i:
                    for p in range(2, 5):
                        pair(p, i)
                pe.wait_ge(s_done, PAIRS * f + PAIRS - 2)
                if f == 0:
                    pe.wait_ge(mod_ready, GM)
                else:
                    pe.wait_ge(mod_ready, MODS)
                out_unit(0)
                out_unit(1)
                pe.wait_ge(s_done, PAIRS * f + PAIRS)
                with pe.Fori(0, (PAIRS - 4) // 3) as i:
                    for u in range(2, 5):
                        out_unit(u, i)
                for u in range((PAIRS - 4) // 3 * 3 + 2, PAIRS - 1):
                    out_unit(u)
                out_unit(PAIRS - 1)

            def scores(i):
                pe.wait_ge(q_copied, i + 1)
                pe.wait_ge(k_copied, i + 1)
                for h in range(2):
                    pe.matmul(ps[:, 3 + h, 0:256], qT[:, h, 128:256], kTt[:, h, :], start=True, stop=True)
                    ins = pe.matmul(ps[:, 3 + h, 256:384], qT[:, h, 0:128], kTt[:, h, 0:128], start=True, stop=True)
                ins.then_inc(scores_done, 1)

            def turn(i):
                pe.wait_ge(probs_ready, i + 1)
                pe.wait_ge(v_copied, i + 1)
                for h in range(2):
                    for b, src in enumerate((256, 0, 128)):
                        pe.transpose(ps[:, 5 + h, P * b:P * b + P], probs[:, h, src:src + P], ident[:])
                for h in range(2):
                    for s in range(2):
                        at = (2 * h + s) * P
                        ins = pe.transpose(ps[:, 7, at:at + P], vT[:, h, s * P:s * P + P], ident[:])
                ins.then_inc(probs_turned, 1)

            def values(i):
                pe.wait_ge(probsT_ready, i + 1)
                pe.wait_ge(v_ready, i + 1)
                for h in range(2):
                    pe.matmul(ps[:, 7, T * h + P:T * h + T], v_tok[:, h, 1, :], probsT[:, h, 256:384],
                              start=True, stop=False, skip_group_check=True)
                    ins = pe.matmul(ps[:, 7, T * h:T * h + T], v_tok[:, h, 0, :], probsT[:, h, 0:256],
                                    start=False, stop=True, skip_group_check=True)
                ins.then_inc(pv_done, 1)

            def attention(i, first):
                n, r = U_QKV, (0 if first else i)
                if not first:
                    pe.wait_ge(q_copied, i)
                col_unit(n, 0, r, 3, KT if first else None)
                if first:
                    pe.wait_ge(dtw_lo, 1)
                    pe.wait_ge(toep_ready, 4)
                    for s in range(2):
                        for k in range(KT):
                            at = slice(s * P, s * P + P)
                            dst = ps[:, 5, SH * s:SH * s + SH]
                            pe.matmul(dst, u_high[:, k, at], dtw_high[:, k, :], start=(k == 0), stop=False,
                                      skip_group_check=True)
                            pe.matmul(dst, u_high[:, k, at], dtw_low[:, k, :], start=False, stop=False,
                                      skip_group_check=True)
                            ins = pe.matmul(dst, u_low[:, k, at], dtw_high[:, k, :], start=False, stop=(k == KT - 1),
                                            skip_group_check=True)
                    ins.then_inc(dt_done, 1)
                else:
                    pe.wait_ge(k_copied, i)
                col_unit(n + 1, 1, r, 3)
                if first:
                    pe.wait_ge(mod_ready, SH2 + 1)
                else:
                    turn(i - 1)
                    pe.wait_ge(v_copied, i)
                col_unit(n + 2, 2, r, 3)
                if first:
                    pe.wait_ge(dt_ready, 1)
                    da = dts[:, 2]
                    pe.matmul(ps[:, 5, 2 * SH:3 * SH], mask[:, 0:P], da[:, 0, :], start=True, stop=True)
                    pe.matmul(ps[:, 5, 3 * SH:4 * SH], ones[:], da[:, 0, :], start=True, stop=False,
                              skip_group_check=True)
                    pe.matmul(ps[:, 5, 3 * SH:4 * SH], mask[:, 0:P], da[:, 1, :], start=False, stop=True,
                              skip_group_check=True).then_inc(cum_done, 1)
                scores(i)
                if first:
                    pe.wait_ge(cum_copied, 1)
                    pe.transpose(ps[0:SH, 6, 0:P], cum[:, 0, :], ident[:])
                    pe.transpose(ps[0:SH, 6, P:2 * P], cum[:, 1, :], ident[:]).then_inc(cum_turned, 1)
                else:
                    values(i - 1)

            def stage_in(g):
                pe.wait_ge(conv_silu, 2 * g + 2)
                for s in range(2):
                    for q in range(2):
                        at = 256 * s + P * q
                        pe.transpose(ps[:, 4, at:at + P], conv[:, q, s * P:s * P + P], ident[:])
                pe.matmul(ps[:, 3, 0:T], conv[:, 2, 0:P], conv[:, 3, :], start=True, stop=True)
                pe.matmul(ps[:, 3, T:T + P], conv[:, 2, P:T], conv[:, 3, P:T], start=True,
                          stop=True).then_inc(ssd_in, 1)
                if isinstance(g, int) and g == 0:
                    pe.wait_ge(cum_lo, 1)
                pe.wait_ge(sel_ready, g + 1)
                for j in range(HG):
                    dst = ps[:, 5 + j // 2, T * (j % 2):T * (j % 2) + T]
                    pe.matmul(dst, sel[:, j, :], cum_high[:], start=True, stop=False, skip_group_check=True)
                    ins = pe.matmul(dst, sel[:, j, :], cum_low[:], start=False, stop=True, skip_group_check=True)
                ins.then_inc(ssd_cum, 1)

            def stage_y(g):
                pe.wait_ge(w_ready, g + 1)
                pe.wait_ge(xdt_ready, g + 1)
                for j in range(HG):
                    half, at = 64 * (j % 2), T * (j // 2)
                    pe.matmul(ps[half:half + HP, 7, at + P:at + T], xdt[:, 1, j, :], decay[:, j, T:384],
                              start=True, stop=False, skip_group_check=True)
                    ins = pe.matmul(ps[half:half + HP, 7, at:at + T], xdt[:, 0, j, :], decay[:, j, 0:T],
                                    start=False, stop=True, skip_group_check=True)
                ins.then_inc(y_done, 1)

            def stage_mean(g):
                pe.wait_ge(g_summed, g + 1)
                pe.wait_ge(y_skip, g + 1)
                pe.matmul(ps[:, 7, 0:T], ones_g[:], gsq[:, 0, :], start=True, stop=True).then_inc(g_mean, 1)

            def ssm(g):
                count = g if isinstance(g, int) else 2
                n = U_SSD
                if count == 0:
                    pe.wait_ge(q_copied, H // 2)
                else:
                    pe.wait_ge(conv_done, 2 * g - 1)
                col_unit(n, 0, g, 3)
                if count == 0:
                    turn(H // 2 - 1)
                    pe.wait_ge(k_copied, H // 2)
                else:
                    pe.wait_ge(conv_done, 2 * g)
                col_unit(n + 1, 1, g, 3)
                if count == 0:
                    values(H // 2 - 1)
                    pe.wait_ge(v_copied, H // 2)
                if count == 1:
                    pe.wait_ge(o_lo, H // 2)
                if count == 2:
                    pe.wait_ge(g_rms, g - 1)
                if count >= 1:
                    stage_y(g - 1)
                    pe.wait_ge(z_silu, g)
                col_unit(n + 2, 2, g, 3)
                if count >= 1:
                    pe.wait_ge(cbm_ready, g)
                    pe.wait_ge(xdt_ready, g)
                    pe.wait_ge(seg_done, g)
                else:
                    pe.wait_ge(o_lo, H // 2)
                stage_in(g)
                if count >= 1:
                    stage_mean(g - 1)

            pe.wait_ge(const_loaded, 16)
            pe.wait_ge(c_loaded, 16)
            pe.transpose(ps[:, 4, 0:KT], par[0:KT, 0, :], ident[0:KT, 0:KT]).then_inc(c_turned, 1)
            pe.wait_ge(x_loaded, 16)
            x_tok = work[:].rearrange("p k t -> p (k t)").rearrange("p (s d) -> p s d", s=2)
            for k in range(KT):
                for s in range(2):
                    at = T * (k % 2) + P * s
                    ins = pe.transpose(ps[:, k // 2, at:at + P], x_tok[:, s, k * P:k * P + P], ident[:])
                if k % 2 == 1:
                    ins.then_inc(x_turned, 1)
            pe.wait_ge(ones_set, 4)
            for k in range(KT):
                pe.wait_ge(squared, k // 2 + 1)
                ins = pe.matmul(ps[:, 6, 0:T], ones_d[:], work[:, k, :], start=(k == 0), stop=(k == KT - 1))
            ins.then_inc(mean_done, 1)
            pe.wait_ge(onehot_loaded, 3 * 16)
            pe.matmul(ps[0:H, 5, 0:384], rel_tab[:], onehot, start=True, stop=True).then_inc(bias_made, 1)
            pe.wait_ge(par_loaded, 7 * 16)
            pe.wait_ge(cs_ready, 1)
            pe.transpose(ps[:, 4, 0:P], par[:, 0, :], ident[:]).then_inc(par_turned, 1)
            ada_sum(0, 7)
            pe.wait_ge(mod_ready, 1)
            ada_sum(1, 7)
            ffn(0, U_F1IN, U_F1OUT)
            mean(1, 0)
            ada_sum(GM, 2)
            ada_sum(SH2, 3)
            mean(2, 1)
            pe.wait_ge(hankel_loaded, 16)
            for b in range(4):
                ins = pe.matmul(ps[:, 4 + b, :], flip[:], hankel[:, 2 * b:2 * b + 2, :], start=True, stop=True)
            ins.then_inc(toep_turned, 1)
            attention(0, True)
            with pe.Fori(1, H // 2) as i:
                attention(i, False)
            ssm(0)
            ssm(1)
            with pe.Fori(2, G) as g:
                ssm(g)
            for u in range(4):
                if u == 0:
                    pe.wait_ge(conv_done, 2 * G - 1)
                if u == 1:
                    pe.wait_ge(conv_done, 2 * G)
                if u == 2:
                    pe.wait_ge(seg_done, G)
                col_unit(U_GA + u, GA_BANK[u])
                if u == 1:
                    pe.wait_ge(g_rms, G - 1)
                    stage_y(G - 1)
                if u == 3:
                    stage_mean(G - 1)
            pe.wait_ge(gate_a_done, 2)
            pe.wait_ge(z_silu, G)
            pe.wait_ge(cbm_ready, G)
            for u in range(4):
                row_unit(U_PA + u, 0, 2 * u, u == 0, u == 3)
            pe.wait_ge(xdt_ready, G)
            pe.wait_ge(gate_a_done, 4)
            pe.wait_ge(g_rms, G)
            for u in range(8):
                pe.wait_ge(g_lo, u + 1)
                row_unit(U_PB + u, 4, 8 + 2 * u, u == 0, u == 7)
            pe.wait_ge(mixed_a, 4)
            for u in range(4):
                if u >= 2:
                    pe.wait_ge(gate_b_done, u - 1)
                col_unit(U_GB + u, u % 2)
            pe.wait_ge(gate_b_used, 2)
            for u in range(4):
                pe.wait_ge(m_lo, u + 1)
                row_unit(U_WO + u, 2, 2 * u, u == 0, u == 3, completes=(u == 3))
            pe.wait_ge(gate_b_done, 4)
            mean(3, 0)
            pe.wait_ge(gate_b_used, 4)
            ada_sum(SC2, 6)
            ada_sum(G2, 7)
            mean(4, 1)
            ffn(1, U_F2IN, U_F2OUT)
            mean(5, 0)
            pe.wait_ge(rms_ready, 6)
            for b in range(4):
                pe.wait_ge(h_early if b < 2 else h_late, 4 + b % 2 + 1)
                for k in range(2):
                    for s in range(2):
                        ins = pe.transpose(ps[:, b, T * s + P * k:T * s + P * k + P],
                                           hT[:, 2 * b + k, s * P:s * P + P], ident[:])
                ins.then_inc(out_turned, 1)


_INS = ['x', 'c', 'w_ada', 'b_ada', 'ffn1_norm_pre', 'ffn1_w_in', 'ffn1_w_out', 'ffn1_norm_post', 'mix_norm_pre',
        'w_in_mix', 'rel_bias', 'conv_w', 'conv_b', 'dt_bias', 'a_log', 'd_skip', 'ssm_norm_w', 'proj_a', 'proj_b',
        'w_out_mix', 'mix_norm_post', 'ffn2_norm_pre', 'ffn2_w_in', 'ffn2_w_out', 'ffn2_norm_post']


def constants():
    m = np.arange(384)
    rel = (T - 1) - m
    dist = np.maximum(rel, 0)
    exact = BUCKETS // 2
    large = exact + (np.log(np.maximum(dist, 1) / exact) / np.log(128 / exact) * (BUCKETS - exact)).astype(np.int64)
    bucket = np.where(dist < exact, dist, np.minimum(large, BUCKETS - 1))
    upper = np.triu(np.ones((P, P), np.float32))
    return {
        'k_ident': np.eye(P, dtype=np.float32),
        'k_flip': np.eye(P, dtype=np.float32)[::-1].copy(),
        'k_mask': np.concatenate([upper, np.ones((P, P), np.float32), upper], axis=1),
        'k_onehot': (np.arange(BUCKETS)[:, None] == bucket[None, :]).astype(np.float32),
        'k_causal': np.broadcast_to(np.where(rel < 0, NEG, 0.0).astype(np.float32), (H, 384)).copy(),
    }


def kernel(**inputs):
    import concourse.bacc as bacc
    from concourse.bass_utils import run_bass_kernel_spmd

    nc = bacc.Bacc("TRN2", target_bir_lowering=False, num_devices=1)
    arrays = {name: np.ascontiguousarray(inputs[name]) for name in _INS}
    arrays.update(constants())
    a = {name: nc.dram_tensor(f"in_{name}", v.shape, mybir.dt.from_np(v.dtype), kind="ExternalInput").ap()
         for name, v in arrays.items()}
    out = nc.dram_tensor("out_0", (1, T, D), F32, kind="ExternalOutput").ap()
    bias_rows = nc.dram_tensor("bias_rows", (H, 384), F32, kind="Internal").ap()
    build(nc, a['x'], a['c'], a['w_ada'], a['b_ada'],
          [a[n] for n in ('ffn1_norm_pre', 'ffn1_norm_post', 'mix_norm_pre', 'mix_norm_post', 'ffn2_norm_pre',
                          'ffn2_norm_post')],
          [a['ffn1_w_in'][0], a['ffn2_w_in'][0]], [a['ffn1_w_out'][0], a['ffn2_w_out'][0]], a['w_in_mix'],
          a['rel_bias'], a['conv_w'], a['conv_b'], a['dt_bias'], a['a_log'], a['d_skip'], a['ssm_norm_w'],
          a['proj_a'], a['proj_b'], a['w_out_mix'], a['k_ident'], a['k_flip'], a['k_mask'], a['k_onehot'],
          a['k_causal'], bias_rows, out)
    r = run_bass_kernel_spmd(nc, [{f"in_{n}": v for n, v in arrays.items()}], core_ids=[0])
    return r.results[0]["out_0"]
```
